# Optimizing a Trainium2 kernel written in Bass

```python
import math
import jax, jax.numpy as jnp
from jax import lax
import numpy as np

D_MODEL = 1024
BATCH = 1
SEQ = 1024
DEPTH = 1

GLA_HEADS = 4
GLA_DK = 128
GLA_DV = 256
GLA_GATE_RANK = 16
GLA_TAU = 16.0
GLA_CHUNK = 64

MLA_HEADS = 8
MLA_Q_RANK = 384
MLA_KV_RANK = 256
MLA_NOPE = 128
MLA_ROPE = 64
MLA_V = 128
ROPE_THETA = 10000.0
ATTN_BLOCK = 128

D_FF = 2816
CONV_WIDTH = 3

DN_ALPHA = (2.0 * DEPTH) ** 0.25
DN_BETA = (8.0 * DEPTH) ** -0.25
LN_EPS = 1e-5
RMS_EPS = 1e-6

IN_SPLITS = (
    GLA_HEADS * GLA_DK,
    GLA_HEADS * GLA_DK,
    GLA_HEADS * GLA_DV,
    GLA_GATE_RANK,
    GLA_HEADS * GLA_DV,
    MLA_Q_RANK,
    MLA_KV_RANK,
    MLA_ROPE,
    D_MODEL,
    D_MODEL,
)
D_IN = sum(IN_SPLITS)

kernel_name = "hybrid_gla_mla_convffn_deepnorm"

def _rmsnorm(x, g):
    xf = x.astype(jnp.float32)
    y = xf * lax.rsqrt(jnp.mean(xf * xf, axis=-1, keepdims=True) + RMS_EPS)
    return (y * g.astype(jnp.float32)).astype(x.dtype)

def _layernorm(x, g, b):
    xf = x.astype(jnp.float32)
    mu = jnp.mean(xf, axis=-1, keepdims=True)
    xc = xf - mu
    var = jnp.mean(xc * xc, axis=-1, keepdims=True)
    y = xc * lax.rsqrt(var + LN_EPS) * g.astype(jnp.float32) + b.astype(jnp.float32)
    return y.astype(x.dtype)

def _rope_tables(positions):
    half = MLA_ROPE // 2
    inv_freq = ROPE_THETA ** (-jnp.arange(half, dtype=jnp.float32) / half)
    ang = positions.astype(jnp.float32)[..., None] * inv_freq
    return jnp.cos(ang), jnp.sin(ang)

def _rope(x, cos, sin):
    half = MLA_ROPE // 2
    xf = x.astype(jnp.float32)
    x1, x2 = xf[..., :half], xf[..., half:]
    out = jnp.concatenate([x1 * cos - x2 * sin, x2 * cos + x1 * sin], axis=-1)
    return out.astype(x.dtype)

def _gla_chunked(q, k, v, log_a):
    B, S, H, DK = q.shape
    DV = v.shape[-1]
    C = GLA_CHUNK
    N = S // C

    def chunk(t):
        return t.astype(jnp.float32).reshape(B, N, C, H, t.shape[-1]).transpose(1, 0, 3, 2, 4)

    qc = chunk(q) * (DK ** -0.5)
    kc = chunk(k)
    vc = chunk(v)
    b = jnp.cumsum(chunk(log_a), axis=3)
    b_last = b[:, :, :, -1:, :]
    q_in = qc * jnp.exp(b)
    k_in = kc * jnp.exp(-b)
    k_st = kc * jnp.exp(b_last - b)
    decay = jnp.exp(b_last[:, :, :, 0, :])

    causal = jnp.tril(jnp.ones((C, C), dtype=bool))
    att = jnp.einsum('nbhid,nbhjd->nbhij', q_in, k_in)
    att = jnp.where(causal, att, 0.0)
    o_intra = jnp.einsum('nbhij,nbhjv->nbhiv', att, vc)

    def step(state, inp):
        q_n, k_n, v_n, d_n = inp
        o_n = jnp.einsum('bhid,bhdv->bhiv', q_n, state)
        state = state * d_n[..., None] + jnp.einsum('bhjd,bhjv->bhdv', k_n, v_n)
        return state, o_n

    s0 = jnp.zeros((B, H, DK, DV), jnp.float32)
    _, o_inter = lax.scan(step, s0, (q_in, k_st, vc, decay))
    o = o_intra + o_inter
    return o.transpose(1, 0, 3, 2, 4).reshape(B, S, H, DV)

def _mla_attention(q_nope, q_rope, k_nope, k_rope, v):
    B, S, H, _ = q_nope.shape
    nblk = S // ATTN_BLOCK
    scale = (MLA_NOPE + MLA_ROPE) ** -0.5
    key_pos = jnp.arange(S)

    def blocks(t):
        return t.reshape((B, nblk, ATTN_BLOCK) + t.shape[2:]).swapaxes(0, 1)

    def attend(args):
        qn, qr, blk = args
        s = (jnp.einsum('bqhd,bkhd->bhqk', qn, k_nope)
             + jnp.einsum('bqhr,bkr->bhqk', qr, k_rope)).astype(jnp.float32) * scale
        q_pos = blk * ATTN_BLOCK + jnp.arange(ATTN_BLOCK)
        mask = key_pos[None, :] <= q_pos[:, None]
        s = jnp.where(mask, s, -jnp.inf)
        p = jax.nn.softmax(s, axis=-1).astype(v.dtype)
        return jnp.einsum('bhqk,bkhv->bqhv', p, v)

    out = lax.map(attend, (blocks(q_nope), blocks(q_rope), jnp.arange(nblk)))
    return out.swapaxes(0, 1).reshape(B, S, H * MLA_V)

def setup_inputs(seed: int = 0) -> dict:
    key = jax.random.key(seed)
    ks = jax.random.split(key, 24)
    f32 = jnp.float32
    L = DEPTH

    def w(k, shape, fan_in, scale=1.0):
        return jax.random.normal(k, shape, f32) * (scale * fan_in ** -0.5)

    def gain(k, shape):
        return 1.0 + 0.02 * jax.random.normal(k, shape, f32)

    def bias(k, shape):
        return 0.02 * jax.random.normal(k, shape, f32)

    x = jax.random.normal(ks[0], (BATCH, SEQ, D_MODEL), f32)
    offs = jax.random.randint(ks[1], (BATCH, 1), 0, 4096, dtype=jnp.int32)
    positions = (offs + jnp.arange(SEQ, dtype=jnp.int32)[None, :]).astype(jnp.int32)
    return {
        "x": x,
        "positions": positions,
        "w_in": w(ks[2], (L, D_MODEL, D_IN), D_MODEL),
        "gla_w_gate_up": w(ks[3], (L, GLA_GATE_RANK, GLA_HEADS * GLA_DK), GLA_GATE_RANK),
        "gla_b_gate": bias(ks[4], (L, GLA_HEADS * GLA_DK)),
        "gla_norm_g": gain(ks[5], (L, GLA_DV)),
        "w_gla_o": w(ks[6], (L, GLA_HEADS * GLA_DV, D_MODEL), GLA_HEADS * GLA_DV),
        "mla_q_norm_g": gain(ks[7], (L, MLA_Q_RANK)),
        "mla_w_uq": w(ks[8], (L, MLA_Q_RANK, MLA_HEADS * (MLA_NOPE + MLA_ROPE)), MLA_Q_RANK),
        "mla_kv_norm_g": gain(ks[9], (L, MLA_KV_RANK)),
        "mla_w_ukv": w(ks[10], (L, MLA_KV_RANK, MLA_HEADS * (MLA_NOPE + MLA_V)), MLA_KV_RANK),
        "w_mla_o": w(ks[11], (L, MLA_HEADS * MLA_V, D_MODEL), MLA_HEADS * MLA_V),
        "w_out": w(ks[12], (L, D_MODEL, D_MODEL), D_MODEL, DN_BETA),
        "ln1_g": gain(ks[13], (L, D_MODEL)),
        "ln1_b": bias(ks[14], (L, D_MODEL)),
        "w_up": w(ks[15], (L, D_MODEL, 2 * D_FF), D_MODEL),
        "conv_w": w(ks[16], (L, CONV_WIDTH, 2 * D_FF), CONV_WIDTH),
        "conv_b": bias(ks[17], (L, 2 * D_FF)),
        "w_down": w(ks[18], (L, D_FF, D_MODEL), D_FF, DN_BETA),
        "ln2_g": gain(ks[19], (L, D_MODEL)),
        "ln2_b": bias(ks[20], (L, D_MODEL)),
    }

def reference(x, positions, w_in, gla_w_gate_up, gla_b_gate, gla_norm_g, w_gla_o,
              mla_q_norm_g, mla_w_uq, mla_kv_norm_g, mla_w_ukv, w_mla_o, w_out,
              ln1_g, ln1_b, w_up, conv_w, conv_b, w_down, ln2_g, ln2_b):
    B, S, D = x.shape
    offsets = []
    acc = 0
    for n in IN_SPLITS[:-1]:
        acc += n
        offsets.append(acc)
    cos, sin = _rope_tables(positions)
    cos_h, sin_h = cos[:, :, None, :], sin[:, :, None, :]

    h = x
    for l in range(DEPTH):
        proj = h @ w_in[l]
        (g_q, g_k, g_v, g_r, g_og, m_cq, m_ckv, m_kr, gate_a, gate_b) = jnp.split(proj, offsets, axis=-1)

        gate_logit = (g_r @ gla_w_gate_up[l] + gla_b_gate[l]).astype(jnp.float32)
        log_a = jax.nn.log_sigmoid(gate_logit) / GLA_TAU
        o = _gla_chunked(g_q.reshape(B, S, GLA_HEADS, GLA_DK),
                         g_k.reshape(B, S, GLA_HEADS, GLA_DK),
                         g_v.reshape(B, S, GLA_HEADS, GLA_DV),
                         log_a.reshape(B, S, GLA_HEADS, GLA_DK)).astype(h.dtype)
        o = _rmsnorm(o, gla_norm_g[l]).reshape(B, S, GLA_HEADS * GLA_DV)
        y_gla = (o * jax.nn.silu(g_og)) @ w_gla_o[l]

        c_q = _rmsnorm(m_cq, mla_q_norm_g[l])
        q = (c_q @ mla_w_uq[l]).reshape(B, S, MLA_HEADS, MLA_NOPE + MLA_ROPE)
        q_nope = q[..., :MLA_NOPE]
        q_rope = _rope(q[..., MLA_NOPE:], cos_h, sin_h)
        c_kv = _rmsnorm(m_ckv, mla_kv_norm_g[l])
        kv = (c_kv @ mla_w_ukv[l]).reshape(B, S, MLA_HEADS, MLA_NOPE + MLA_V)
        k_nope = kv[..., :MLA_NOPE]
        v = kv[..., MLA_NOPE:]
        k_rope = _rope(m_kr, cos, sin)
        y_mla = _mla_attention(q_nope, q_rope, k_nope, k_rope, v) @ w_mla_o[l]

        mixed = (jax.nn.sigmoid(gate_a) * y_gla + jax.nn.sigmoid(gate_b) * y_mla) @ w_out[l]
        h = _layernorm(DN_ALPHA * h + mixed, ln1_g[l], ln1_b[l])

        u = h @ w_up[l]
        u = lax.conv_general_dilated(
            u, conv_w[l][:, None, :].astype(u.dtype), window_strides=(1,),
            padding=[(CONV_WIDTH - 1, 0)],
            dimension_numbers=('NWC', 'WIO', 'NWC'),
            feature_group_count=2 * D_FF) + conv_b[l]
        u_gate, u_val = u[..., :D_FF], u[..., D_FF:]
        f = (jax.nn.silu(u_gate) * u_val) @ w_down[l]
        h = _layernorm(DN_ALPHA * h + f, ln2_g[l], ln2_b[l])
    return h


_drawn_inputs = setup_inputs


def setup_inputs(seed=0):
    import zlib

    import numpy as np

    out = dict(_drawn_inputs(seed))
    spreads = {}
    factors = {'gla_w_gate_up': 3.326,
     'gla_b_gate': 21.68,
     'gla_norm_g': 43.037,
     'mla_q_norm_g': 8.0,
     'mla_kv_norm_g': 8.0,
     'ln1_b': 2.749,
     'conv_b': 6.995,
     'ln2_g': 8.036,
     'ln2_b': 8.359}
    for name, (base, spread) in spreads.items():
        noise = np.random.default_rng([zlib.crc32(name.encode()), seed]).standard_normal(out[name].shape)
        drawn = base * np.exp(spread * noise) if base else spread * noise
        out[name] = __import__('jax').numpy.asarray(drawn.astype(out[name].dtype))
    for name, factor in factors.items():
        out[name] = (out[name] * factor).astype(out[name].dtype)
    return out
```

```python
from contextlib import ExitStack

import concourse.bass as bass
from concourse import mybir

F32 = mybir.dt.float32
F32R = mybir.dt.float32r
I32 = mybir.dt.int32
ALU = mybir.AluOpType
ACT = mybir.ActivationFunctionType
AX = mybir.AxisListType.X

P = 128
HALF = 512
D, S = 1024, 1024
KT, TT = D // P, S // P
GH, DK, DV, RANK, TAU, CHUNK = 4, 128, 256, 16, 16.0, 64
MH, QR, KR, NOPE, ROPE, MV = 8, 384, 256, 128, 64, 128
QKT, KVT = QR // P, KR // P
DFF = 2816
FT = DFF // P
HR = ROPE // 2
THETA = 10000.0
ALPHA = 2.0 ** 0.25
LN_EPS, RMS_EPS = 1e-5, 1e-6
ATT_SCALE = (NOPE + ROPE) ** -0.5
C_Q = 0
C_K = C_Q + GH * DK
C_V = C_K + GH * DK
C_R = C_V + GH * DV
C_OG = C_R + RANK
C_CQ = C_OG + GH * DV
C_KR = C_CQ + QR + KR
C_GA = C_KR + ROPE
C_GB = C_GA + D
CW = QR + KR + ROPE
LAT = [(0, 240), (240, 240), (480, CW - 480)]
CHUNKS = S // CHUNK
PI = 3.141592653589793


class Chain:

    def __init__(self, eng, sem):
        self.eng, self.sem, self.n = eng, sem, 0

    def done(self, ins):
        ins.then_inc(self.sem, 1)
        self.n += 1
        return self.n

    def wait(self, value=None):
        self.eng.wait_ge(self.sem, self.n if value is None else value)


def block_kernel(nc, x, positions, w_in, gla_w_gate_up, gla_b_gate, gla_norm_g, w_gla_o, mla_q_norm_g,
                 mla_w_uq, mla_kv_norm_g, mla_w_ukv, w_mla_o, w_out, ln1_g, ln1_b, w_up, conv_w, conv_b,
                 w_down, ln2_g, ln2_b, out):
    ctx = ExitStack()
    with ctx:
        def sem(name):
            return ctx.enter_context(nc.semaphore(name))

        def dram(name, shape):
            return nc.dram_tensor(name, shape, F32, kind="Internal").ap()

        psum_all = ctx.enter_context(nc.psum_tensor("psum_all", [P, 8 * HALF], F32))
        psum = [psum_all[:, i * HALF:(i + 1) * HALF] for i in range(8)]

        class Region:

            def __init__(self, start, size):
                self.at, self.end = start, start + size

            def __call__(self, name, shape, dt=F32):
                size = 4
                for s in shape[1:]:
                    size *= s
                t = nc.alloc_sbuf_tensor_at(name, list(shape), dt, offset=self.at)
                self.at += -(-size // 32) * 32
                assert self.at <= self.end, (name, self.at, self.end)
                return t

        KB = 1024
        base = 16512
        RSZ = 92 * KB
        W0 = base
        A0 = W0 + 48 * KB
        R0 = A0 + 64 * KB
        C0 = R0 + RSZ
        wreg = Region(W0, 48 * KB)
        w_raw = [wreg(f"w_raw{i}", [P, 2048]) for i in range(2)]
        w_hi = [wreg(f"w_hi{i}", [P, 2048], F32R) for i in range(2)]
        w_lo = [wreg(f"w_lo{i}", [P, 2048], F32R) for i in range(2)]

        creg = Region(C0, 229344 - C0)
        ident = creg("ident", [P, P])
        mask_att = creg("mask_att", [P, P])
        mask_gla = creg("mask_gla", [P, P])
        zero_col = creg("zero_col", [P, 1])
        b_gate = creg("b_gate", [P, GH])
        norm_g = creg("norm_g", [P, 2])
        lat_g = creg("lat_g", [P, QKT + KVT])
        small = creg("small", [P, 64])
        eps_rms = creg("eps_rms", [P, 1])

        areg = Region(A0, 64 * KB)
        xT_hi = areg("xT_hi", [P, KT, S], F32R)
        xT_lo = areg("xT_lo", [P, KT, S], F32R)
        r = Region(R0, RSZ)
        x_tok = [r(f"x_tok{i}", [P, D]) for i in range(TT)]
        r = Region(R0, RSZ)
        q_raw = r("q_raw", [P, S])
        k_raw = r("k_raw", [P, S])
        gb_b = r("gb_b", [P, S])
        gb_e = r("gb_e", [P, S])
        gb_n = r("gb_n", [P, S])
        q_x = r("q_x", [P, S])
        k_in = r("k_in", [P, S])
        k_up = r("k_up", [P, S])
        og_s = [r(f"og_s{i}", [P, 2, S]) for i in range(2)]
        v_tok = [r(f"v_tok{i}", [P, TT, DV]) for i in range(2)]
        o_tok = r("o_tok", [P, TT, DV])
        rT = r("rT", [RANK, S])
        sig = [r(f"sig{i}", [P, HALF]) for i in range(2)]
        oT_st = [r(f"oT_st{i}", [P, HALF]) for i in range(2)]
        state = r("state", [P, DV])
        att = [r(f"att{i}", [P, P]) for i in range(2)]
        kst = [r(f"kst{i}", [P, P]) for i in range(2)]
        sq_junk = r("sq_junk", [P, DV])
        ss = small[:, 0:8]
        rs = small[:, 8:16]
        b_last = r("b_last", [P, CHUNKS])
        dec = r("dec", [P, CHUNKS])
        dec2 = r("dec2", [P, TT])
        ones64 = r("ones64", [P, CHUNK])
        w_gate = r("w_gate", [RANK, GH * DK])

        d_og = dram("d_og", [GH * DV, S])
        d_sga = dram("d_sga", [D, S])
        d_sgb = dram("d_sgb", [D, S])
        d_m = dram("d_m", [D, S])
        d_qr = dram("d_qr", [MH, P, S])
        d_om = dram("d_om", [MH * MV, S])
        d_h = dram("d_h", [S, D])

        r = Region(R0, RSZ)
        oT_hi = r("oT_hi", [P, KT, S], F32R)
        oT_lo = r("oT_lo", [P, KT, S], F32R)
        ld_st = [r(f"ld_st{i}", [P, S]) for i in range(2)]
        ga_st = [r(f"ga_st{i}", [P, HALF]) for i in range(2)]
        m_st = [r(f"m_st{i}", [P, HALF]) for i in range(2)]
        gsig = [r(f"gsig{i}", [P, HALF]) for i in range(2)]

        r = Region(R0, RSZ)
        cT_hi = r("cT_hi", [P, QKT + KVT, S], F32R)
        cT_lo = r("cT_lo", [P, QKT + KVT, S], F32R)
        kA = r("kA", [P, S], F32R)
        kB = r("kB", [P, S], F32R)
        top = r.at
        c_tok = r("c_tok", [P, TT, CW])
        cos = r("cos", [P, TT, HR])
        sin = r("sin", [P, TT, HR])
        kst3 = r("kst3", [P, TT, 3 * ROPE])
        rtmp = r("rtmp", [P, TT, HR])
        rtmp2 = r("rtmp2", [P, TT, HR])
        pos_i = r("pos_i", [P, TT], I32)
        ifreq = r("ifreq", [P, HR])
        junk2 = r("junk2", [P, QR])
        gsig2 = [r(f"gsig2_{i}", [P, HALF]) for i in range(2)]
        a = Region(A0, 64 * KB)
        qr_rot = [a(f"qr_rot{i}", [P, MH, ROPE]) for i in range(2)]
        qr_tmp = a("qr_tmp", [P, MH, HR])
        qr_tmp2 = a("qr_tmp2", [P, MH, HR])
        qr_hl = [a(f"qr_hl{i}", [P, MH, 2 * ROPE]) for i in range(2)]
        qr_st = [a(f"qr_st{i}", [P, MH, P]) for i in range(2)]
        a = Region(A0, 64 * KB)
        pT_hi = a("pT_hi", [P, TT, HALF], F32R)
        pT_lo = a("pT_lo", [P, TT, HALF], F32R)
        qT = [[a(f"qT{i}{p}", [P, S], F32R) for p in "hl"] for i in range(2)]
        kT = [[a(f"kT{i}{p}", [P, S], F32R) for p in "hl"] for i in range(2)]
        r = Region(top, R0 + RSZ - top)
        vv = [[r(f"vv{i}{p}", [P, TT, MV], F32R) for p in "hl"] for i in range(2)]
        p_sb = [r(f"p_sb{i}", [P, S]) for i in range(2)]
        qrA = [r(f"qrA{i}", [P, S], F32R) for i in range(2)]
        om_st = [r(f"om_st{i}", [P, HALF]) for i in range(2)]
        nmax = r("nmax", [P, 2])
        nbias = r("nbias", [P, 2])
        psums = r("psums", [P, 2])
        prec = r("prec", [P, 2])

        a = Region(A0, 64 * KB)
        mT_hi = a("mT_hi", [P, KT, S], F32R)
        mT_lo = a("mT_lo", [P, KT, S], F32R)
        r = Region(R0, RSZ)
        xm_hi = r("xm_hi", [P, KT, S], F32R)
        xm_lo = r("xm_lo", [P, KT, S], F32R)
        ld2 = [r(f"ld2_{i}", [P, S]) for i in range(2)]
        sgb_st = [r(f"sgb_st{i}", [P, HALF]) for i in range(2)]
        mm_st = [r(f"mm_st{i}", [P, HALF]) for i in range(2)]
        mx = [r(f"mx{i}", [P, HALF]) for i in range(2)]
        a = Region(A0, 64 * KB)
        h_tok = a("h_tok", [P, TT, D])
        ln_g = a("ln1_gain", [P, D])
        ln_b = a("ln1_bias", [P, D])
        bst = a("bst", [P, TT, 12])
        mv = a("mv", [P, TT, 2])
        lrs = a("lrs", [P, TT, 2])
        eps_ln = creg("eps_ln", [P, 1])
        cw = creg("cw", [P, 4, 2 * FT])
        f_all = nc.alloc_sbuf_tensor_at("f_all", [P, FT, S], F32, offset=A0)
        r = Region(R0 + 24 * KB, 68 * KB)
        hT_hi = r("hT_hi", [P, KT, S], F32R)
        hT_lo = r("hT_lo", [P, KT, S], F32R)
        up_g = r("up_g", [P, HALF])
        up_v = r("up_v", [P, HALF])
        cw_rows = nc.alloc_sbuf_tensor_at("cw_rows", [2 * FT, 4, P], F32, offset=R0 + 40 * KB)
        r = Region(R0 + 24 * KB, 68 * KB)
        f_hi = [r(f"f_hi{i}", [P, 2, S], F32R) for i in range(2)]
        f_lo = [r(f"f_lo{i}", [P, 2, S], F32R) for i in range(2)]
        z_tok = r("z_tok", [P, TT, D])
        bst2 = r("bst2", [P, TT, 12])
        mv2 = r("mv2", [P, TT, 2])
        lrs2 = r("lrs2", [P, TT, 2])
        ln2_gt = nc.alloc_sbuf_tensor_at("ln2_gain", [P, D], F32, offset=A0)
        ln2_bt = nc.alloc_sbuf_tensor_at("ln2_bias", [P, D], F32, offset=A0 + 4 * KB)

        win = w_in[0].rearrange("(k p) c -> p k c", p=P)

        def raw(n, k, c):
            return w_raw[n % 2][:, 0:k * c].rearrange("p (k c) -> p k c", k=k)

        slots = []

        def slot(name, k, c, *parts):
            slots.append((name, k, c, parts))

        def win_slot(name, c0, c):
            slot(name, KT, c, (0, c, win[:, :, c0:c0 + c]))

        def head_slots(h):
            win_slot(("og", h), C_OG + h * DV, DV)
            win_slot(("v", h), C_V + h * DV, DV)
            slot(("qk", h), KT, 2 * DK, (0, DK, win[:, :, C_Q + h * DK:C_Q + (h + 1) * DK]),
                 (DK, DK, win[:, :, C_K + h * DK:C_K + (h + 1) * DK]))

        win_slot(("r", 0), C_R, RANK)
        head_slots(0)
        for h in range(GH - 1):
            head_slots(h + 1)
            win_slot(("gb", h), C_GB + h * 256, 256)
        for j in range(4):
            win_slot(("ga", j), C_GA + j * 256, 256)
        for j in range(4):
            slot(("glao", j), KT, 256, (0, 256, w_gla_o[0].rearrange("(k p) c -> p k c", p=P)[:, :, j * 256:(j + 1) * 256]))
        for j, (c0, c) in enumerate(LAT):
            win_slot(("lat", j), C_CQ + c0, c)
        win_slot(("gb", 3), C_GB + 3 * 256, 256)
        uq = mla_w_uq[0].rearrange("(k p) (h c) -> p k h c", p=P, c=NOPE + ROPE)
        ukv = mla_w_ukv[0].rearrange("(k p) (h c) -> p k h c", p=P, c=NOPE + MV)
        slot(("rope", 0), QKT, MH * ROPE, *[(h * ROPE, ROPE, uq[:, :, h, NOPE:]) for h in range(MH)])
        for h in range(MH):
            slots.append((("mla", h), QKT + 2 * KVT, P, (("q", uq[:, :, h, 0:NOPE]), ("k", ukv[:, :, h, 0:NOPE]), ("v", ukv[:, :, h, NOPE:]))))
        for j in range(4):
            slot(("mlao", j), KT, 256, (0, 256, w_mla_o[0].rearrange("(k p) c -> p k c", p=P)[:, :, j * 256:(j + 1) * 256]))
        for j in range(4):
            slot(("wout", j), 4, HALF, (0, HALF, w_out[0].rearrange("(k p) c -> p k c", p=P)[:, j % 2 * 4:j % 2 * 4 + 4, j // 2 * HALF:(j // 2 + 1) * HALF]))
        wup = w_up[0].rearrange("(k p) c -> p k c", p=P)
        for i in range(FT):
            slot(("up", i), KT, 256, (0, P, wup[:, :, i * P:(i + 1) * P]), (P, P, wup[:, :, DFF + i * P:DFF + (i + 1) * P]))
        wdn = w_down[0].rearrange("(k p) c -> p k c", p=P)
        for i in range(FT):
            dh, kk = i // (FT // 2), i % (FT // 2)
            slot(("down", i), 2, HALF, (0, HALF, wdn[:, 2 * kk:2 * kk + 2, dh * HALF:(dh + 1) * HALF]))
        slot_no = {name: n for n, (name, *_) in enumerate(slots)}

        landed_value, total = [], [0, 0]
        for n, (_, k, c, parts) in enumerate(slots):
            total[n % 2] += 16 * len(parts)
            landed_value.append(total[n % 2])

        def w_part(n, k_no, c0, c, lo=False):
            width = slots[n][2]
            t = (w_lo if lo else w_hi)[n % 2]
            return t[:, k_no * width + c0:k_no * width + c0 + c]

        w_landed = [sem("w_landed0"), sem("w_landed1")]
        w_high = sem("w_high")
        w_split = sem("w_split")
        w_used = sem("w_used")
        consts = sem("consts")
        x_landed = [sem(f"x_landed{t}") for t in range(TT)]
        par_landed = sem("par_landed")
        xt_done = sem("xt_done")
        xt_hi = sem("xt_hi")
        xt_lo = sem("xt_lo")
        mm = sem("mm")
        ev_a = sem("ev_a")
        ev_v = sem("ev_v")
        vs = sem("vs")
        as_ = sem("as")

        groups, gid = [], {}

        def group(kind, ev):
            gid[kind] = len(groups)
            groups.append(ev)

        def q4(kind, ev):
            for j in range(4):
                group(kind + (j,), ev)

        for j in range(2):
            group(("r", j), "a")
        q4(("og", 0), "v")
        q4(("v", 0), "a")
        q4(("qk", 0), "a")
        for h in range(GH):
            last = h == GH - 1
            q4(("ga", 0) if last else ("og", h + 1), "a" if last else "v")
            q4(("ga", 1) if last else ("v", h + 1), "a")
            if not last:
                q4(("qk", h + 1), "a")
            q4(("oT", h), "v")
            if not last:
                q4(("gb", h), "a")
        q4(("ga", 2), "a")
        q4(("ga", 3), "a")
        for j in range(4):
            q4(("glao", j), "v")
        for j in range(3):
            for t in range(TT):
                group(("lat", j, t), "a")
        q4(("gb", 3), "a")
        for c in range(QKT + KVT):
            for half in range(2):
                group(("cT", c, half), "v")
        for m in range(2):
            for half in range(2):
                group(("kT", m, half), "a")
        for t in range(TT + 1):
            if t < TT:
                group(("qr", t), "v")
            if t > 0:
                group(("qrT", t - 1, 0), "a")
                group(("qrT", t - 1, 1), "a")
        ev_at, cnt = [], {"a": 0, "v": 0}
        for ev in groups:
            cnt[ev] += 1
            ev_at.append(({"a": ev_a, "v": ev_v}[ev], cnt[ev]))

        def bank(kind):
            return psum[gid[kind] % 4]

        PARAMS = 9

        names = ("gate_mm gate_l gate_scan gate_exp prep_done att_mm att_ok kst_ok ou_mm o_ev st_ev norm_v norm_s "
                 "o_scaled sig_ok lat_sq lat_v lat_s lat_ok hi_ok op_hi op_lo ld_ok rope_q rot_ok kst3_ok sins "
                 "angs s_mm nb_ok p_exp p_norm t_mm pt_hi pt_lo pv_mm om_ev pj_mm pj_hi pj_lo mo_mm mo_ev mix_ok "
                 "mix_hi mix_lo wo_mm wo_ev ln_v ln_s ln_ok hT_mm hT_hi hT_lo up_mm up_a up_v up_c up_si up_f fs_hi fs_lo "
                 "dn_mm dn_ev ln2_v ln2_s ln2_ok ad2 vd2 ifr par_mm par_ok og_stored ga_stored m_stored qr_stored "
                 "om_stored h_stored out_stored pos_ok").split()
        sm = {n: sem(n) for n in names}
        sig_st = [sem("sig_st0"), sem("sig_st1")]
        ld_in = [sem("ld_in0"), sem("ld_in1")]
        ga_in = [sem("ga_in0"), sem("ga_in1")]
        m_out = [sem("m_out0"), sem("m_out1")]
        oT_out = [sem("oT_out0"), sem("oT_out1")]
        qs_out = [sem("qs_out0"), sem("qs_out1")]
        qrA_in = [sem("qrA_in0"), sem("qrA_in1")]
        om_out = [sem("om_out0"), sem("om_out1")]
        mx_in = [sem("mx_in0"), sem("mx_in1")]
        row_in = [sem(f"row_in{t}") for t in range(TT)]
        row2_in = [sem(f"row2_in{t}") for t in range(TT)]
        ln1_in, ln2_in = sem("ln1_in"), sem("ln2_in")

        def tgroup(s, g=0):
            h, qb = divmod(s, TT)
            return 12 * h + (qb if qb < 4 else 4 + 2 * (qb - 4)) + g

        STEPS = MH * TT
        LASTG = {"r": 1, "og": 3, "v": 3, "qk": 3, "gb": 3, "ga": 3, "glao": 3}

        def used_at(n):
            name, i = slots[n][0]
            if name in LASTG:
                return mm, gid[(name, i, LASTG[name])] + 1 if name != "r" else gid[("r", 1)] + 1
            if name == "lat":
                return mm, gid[("lat", i, TT - 1)] + 1
            if name == "rope":
                return mm, gid[("qr", TT - 1)] + 1
            if name == "mla":
                return sm["pj_mm"], 6 * (i + 1)
            if name == "mlao":
                return sm["mo_mm"], 4 * (i + 1)
            if name == "wout":
                return (sm["wo_mm"], TT * (i // 2 + 1)) if i % 2 else (w_used, i // 2 + 1)
            if name == "up":
                return sm["up_mm"], 4 * (i + 1)
            dh, kk = divmod(i, FT // 2)
            if kk == FT // 2 - 1:
                return sm["dn_mm"], TT * (dh + 1)
            return w_used, 2 + dh * (FT // 2 - 1) + kk + 1

        block = ctx.enter_context(nc.Block())

        @block.sync
        def _(sp):
            for t in range(TT):
                sp.dma_start(x_tok[t][:, :], x[0, t * P:(t + 1) * P, :]).then_inc(x_landed[t], 16)
            for n, (name, k, c, parts) in enumerate(slots):
                if n >= 2:
                    sp.wait_ge(w_split, n - 1)
                if name[0] == "mla":
                    at = 0
                    for what, src in parts:
                        kk = QKT if what == "q" else KVT
                        dst = w_raw[n % 2][:, at * P:(at + kk) * P].rearrange("p (k c) -> p k c", k=kk)
                        sp.dma_start(dst, src).then_inc(w_landed[n % 2], 16)
                        at += kk
                    continue
                for c0, cc, src in parts:
                    sp.dma_start(raw(n, k, c)[:, :, c0:c0 + cc], src).then_inc(w_landed[n % 2], 16)

        @block.gpsimd
        def _(pool):
            ms = Chain(pool, consts)
            ms.done(nc.gpsimd.memset(zero_col[:, :], 0.0))
            ms.done(nc.gpsimd.memset(ident[:, :], 1.0))
            ms.done(nc.gpsimd.memset(mask_att[:, :], 0.0))
            ms.done(nc.gpsimd.memset(mask_gla[:, :], 1.0))
            ms.wait()
            ms.done(nc.gpsimd.affine_select(ident[:, :], ident[:, :], pattern=[[-1, P]], compare_op=ALU.is_equal,
                                            fill=0.0, base=0, channel_multiplier=1))
            ms.done(nc.gpsimd.affine_select(mask_att[:, :], mask_att[:, :], pattern=[[-1, P]], compare_op=ALU.is_ge,
                                            fill=-1e30, base=0, channel_multiplier=1))
            ms.done(nc.gpsimd.affine_select(mask_gla[:, :], mask_gla[:, :], pattern=[[1, P]], compare_op=ALU.is_ge,
                                            fill=0.0, base=0, channel_multiplier=-1))
            ms.wait()
            ms.done(nc.gpsimd.memset(mask_gla[0:CHUNK, CHUNK:P], 0.0))
            ms.done(nc.gpsimd.memset(ones64[:, :], 1.0))
            ms.done(nc.gpsimd.memset(eps_rms[:, :], RMS_EPS))
            ms.done(nc.gpsimd.memset(eps_ln[:, :], LN_EPS))
            for n, (name, k, c, parts) in enumerate(slots):
                w = k * c
                pool.wait_ge(w_landed[n % 2], landed_value[n])
                if n >= 2:
                    pool.wait_ge(*used_at(n - 2))
                nc.gpsimd.tensor_copy(w_hi[n % 2][:, 0:w], w_raw[n % 2][:, 0:w]).then_inc(w_high, 1)
                pool.wait_ge(w_high, n + 1)
                nc.gpsimd.tensor_tensor(w_lo[n % 2][:, 0:w], w_raw[n % 2][:, 0:w],
                                        w_hi[n % 2][:, 0:w].bitcast(F32), ALU.subtract).then_inc(w_split, 1)

        @block.tensor
        def _(pe):
            def free(kind):
                g = gid[kind]
                if g >= 4:
                    pe.wait_ge(*ev_at[g - 4])

            def split3(out_ap, terms, start=True, stop=True):
                for i, (ah, al, bh, bl) in enumerate(terms):
                    pe.matmul(out_ap, ah, bh, start=start and i == 0, stop=False)
                    pe.matmul(out_ap, ah, bl, start=False, stop=False)
                    last = pe.matmul(out_ap, al, bh, start=False, stop=stop and i == len(terms) - 1)
                return last

            def need(name):
                n = slot_no[name]
                pe.wait_ge(w_split, n + 1)
                return n

            def feature_group(kind, n, tile, half, th, tl, kts=KT):
                free(kind)
                last = split3(bank(kind), [(w_part(n, k, tile * P, P), w_part(n, k, tile * P, P, True),
                                            th[:, k, half * HALF:(half + 1) * HALF], tl[:, k, half * HALF:(half + 1) * HALF])
                                           for k in range(kts)])
                last.then_inc(mm, 1)
                return last

            def features(kind, name, th, tl, js=range(4)):
                n = need(name)
                for j in js:
                    feature_group(kind + (j,), n, j // 2, j % 2, th, tl)

            def v_groups(h, js=range(4)):
                n = need(("v", h))
                for j in js:
                    kind = ("v", h, j)
                    free(kind)
                    for i in range(2):
                        t = 2 * j + i
                        last = split3(bank(kind)[:, i * DV:(i + 1) * DV],
                                      [(xT_hi[:, k, t * P:(t + 1) * P], xT_lo[:, k, t * P:(t + 1) * P],
                                        w_part(n, k, 0, DV), w_part(n, k, 0, DV, True)) for k in range(KT)])
                    last.then_inc(mm, 1)

            def transposes(kind, srcs):
                free(kind)
                for i, s_ap in enumerate(srcs):
                    last = pe.transpose(bank(kind)[:, i * P:(i + 1) * P], s_ap, ident[:, :])
                last.then_inc(mm, 1)

            def gates(h):
                if h == 0:
                    pe.wait_ge(par_landed, 16 * PARAMS)
                    pe.wait_ge(*ev_at[gid[("r", 1)]])
                else:
                    pe.wait_ge(sm["att_ok"], TT * h)
                    pe.wait_ge(sm["kst_ok"], TT * h)
                    pe.wait_ge(sm["o_ev"], TT * h)
                for half in range(2):
                    last = pe.matmul(psum[4 + half], w_gate[:, h * DK:(h + 1) * DK], rT[:, half * HALF:(half + 1) * HALF],
                                     start=True, stop=True)
                last.then_inc(sm["gate_mm"], 1)

            def att_part(h, t):
                i = h * TT + t
                c = slice(t * P, (t + 1) * P)
                if i >= 1:
                    pe.wait_ge(sm["att_ok"], i)
                    pe.wait_ge(sm["kst_ok"], i)
                pe.matmul(psum[4][:, 0:P], k_in[:, c], q_raw[:, c], start=True, stop=True)
                pe.matmul(psum[4][0:CHUNK, P:P + CHUNK], k_raw[:, t * P:t * P + CHUNK], q_raw[:, t * P + CHUNK:(t + 1) * P],
                          start=True, stop=True)
                pe.transpose(psum[7][:, 0:P], k_up[:, c], ident[:, :]).then_inc(sm["att_mm"], 1)

            def out_part(h, t):
                i = h * TT + t
                pe.wait_ge(sm["att_ok"], i + 1)
                if i >= 1:
                    pe.wait_ge(sm["o_ev"], i)
                    pe.wait_ge(sm["st_ev"], i)
                pe.matmul(psum[5][:, 0:DV], att[i % 2][:, :], v_tok[h % 2][:, t, :], start=True, stop=t == 0)
                if t > 0:
                    pe.matmul(psum[5][:, 0:DV], q_x[:, t * P:(t + 1) * P], state[:, :], start=False, stop=True)
                pe.wait_ge(sm["kst_ok"], i + 1)
                pe.matmul(psum[6][:, 0:DV], kst[i % 2][:, :], v_tok[h % 2][:, t, :], start=True, stop=True).then_inc(sm["ou_mm"], 1)

            pe.wait_ge(consts, 7)
            for t in range(TT):
                pe.wait_ge(x_landed[t], 16)
                for g in range(2):
                    i = 2 * t + g
                    if i >= 4:
                        pe.wait_ge(xt_lo, i - 3)
                    for j in range(4):
                        last = pe.transpose(psum[i % 4][:, j * P:(j + 1) * P], x_tok[t][:, (4 * g + j) * P:(4 * g + j + 1) * P], ident[:, :])
                    last.then_inc(xt_done, 1)
            pe.wait_ge(par_landed, 16 * PARAMS)
            for k in range(4):
                last = pe.transpose(psum[7][:, k * 2 * FT:(k + 1) * 2 * FT], cw_rows[:, k, :], ident[0:2 * FT, 0:2 * FT])
            last.then_inc(sm["par_mm"], 1)
            pe.wait_ge(xt_lo, 2 * TT)
            n = need(("r", 0))
            for half in range(2):
                kind = ("r", half)
                last = split3(bank(kind)[0:RANK, :], [(w_part(n, k, 0, RANK), w_part(n, k, 0, RANK, True),
                                                       xT_hi[:, k, half * HALF:(half + 1) * HALF], xT_lo[:, k, half * HALF:(half + 1) * HALF])
                                                      for k in range(KT)])
                last.then_inc(mm, 1)
            features(("og", 0), ("og", 0), xT_hi, xT_lo)
            v_groups(0)
            gates(0)
            features(("qk", 0), ("qk", 0), xT_hi, xT_lo)
            for h in range(GH):
                last_head = h == GH - 1
                pe.wait_ge(sm["prep_done"], h + 1)
                pe.wait_ge(*ev_at[gid[("v", h, 3)]])
                for t in range(TT):
                    att_part(h, t)
                    if last_head:
                        features(("ga", t // 4), ("ga", t // 4), xT_hi, xT_lo, [t % 4])
                    elif t < 4:
                        features(("og", h + 1), ("og", h + 1), xT_hi, xT_lo, [t])
                    else:
                        v_groups(h + 1, [t - 4])
                    out_part(h, t)
                if not last_head:
                    gates(h + 1)
                    features(("qk", h + 1), ("qk", h + 1), xT_hi, xT_lo)
                pe.wait_ge(sm["o_scaled"], h + 1)
                for j in range(4):
                    vt, half = divmod(j, 2)
                    transposes(("oT", h, j), [o_tok[:, 4 * half + i, vt * P:(vt + 1) * P] for i in range(4)])
                if not last_head:
                    features(("gb", h), ("gb", h), xT_hi, xT_lo)
            features(("ga", 2), ("ga", 2), xT_hi, xT_lo)
            features(("ga", 3), ("ga", 3), xT_hi, xT_lo)
            pe.wait_ge(sm["op_lo"], KT)
            for j in range(4):
                features(("glao", j), ("glao", j), oT_hi, oT_lo)
            for j, (c0, c) in enumerate(LAT):
                n = need(("lat", j))
                for t in range(TT):
                    kind = ("lat", j, t)
                    free(kind)
                    split3(bank(kind)[:, 0:c], [(xT_hi[:, k, t * P:(t + 1) * P], xT_lo[:, k, t * P:(t + 1) * P],
                                                 w_part(n, k, 0, c), w_part(n, k, 0, c, True)) for k in range(KT)]).then_inc(mm, 1)
            features(("gb", 3), ("gb", 3), xT_hi, xT_lo)
            pe.wait_ge(sm["lat_ok"], 1)
            for c in range(QKT + KVT):
                for half in range(2):
                    transposes(("cT", c, half), [c_tok[:, 4 * half + i, c * P:(c + 1) * P] for i in range(4)])
            pe.wait_ge(sm["kst3_ok"], 1)
            for m in range(2):
                for half in range(2):
                    c0 = ROPE if m == 0 else 0
                    transposes(("kT", m, half), [kst3[:, 4 * half + i, c0:c0 + P] for i in range(4)])
            n = need(("rope", 0))
            pe.wait_ge(*ev_at[gid[("cT", QKT + KVT - 1, 1)]])
            for t in range(TT + 1):
                if t < TT:
                    kind = ("qr", t)
                    free(kind)
                    split3(bank(kind), [(cT_hi[:, k, t * P:(t + 1) * P], cT_lo[:, k, t * P:(t + 1) * P],
                                         w_part(n, k, 0, HALF), w_part(n, k, 0, HALF, True)) for k in range(QKT)]).then_inc(mm, 1)
                if t > 0:
                    pe.wait_ge(sm["rot_ok"], t)
                    for g in range(2):
                        transposes(("qrT", t - 1, g), [qr_hl[(t - 1) % 2][:, 4 * g + i, :] for i in range(4)])

            def project(h, j):
                n = need(("mla", h))
                pe.wait_ge(sm["pj_lo"], 6 * h + j) if 6 * h + j else None
                if j < 4:
                    half, kts, k0, c0 = j % 2, (QKT, KVT)[j // 2], (0, QKT)[j // 2], (0, QKT)[j // 2]
                    last = split3(psum[7], [(w_part(n, c0 + k, 0, P), w_part(n, c0 + k, 0, P, True),
                                             cT_hi[:, k0 + k, half * HALF:(half + 1) * HALF], cT_lo[:, k0 + k, half * HALF:(half + 1) * HALF])
                                            for k in range(kts)])
                else:
                    for i in range(4):
                        t = 4 * (j - 4) + i
                        last = split3(psum[7][:, i * P:(i + 1) * P],
                                      [(cT_hi[:, QKT + k, t * P:(t + 1) * P], cT_lo[:, QKT + k, t * P:(t + 1) * P],
                                        w_part(n, QKT + KVT + k, 0, P), w_part(n, QKT + KVT + k, 0, P, True)) for k in range(KVT)])
                last.then_inc(sm["pj_mm"], 1)
    
            def scores(s):
                h, qb = divmod(s, TT)
                q = slice(qb * P, (qb + 1) * P)
                if qb == 0:
                    pe.wait_ge(sm["pj_lo"], 6 * (h + 1))
                    pe.wait_ge(qrA_in[h % 2], 16 * (h // 2 + 1))
                if s >= 2:
                    pe.wait_ge(sm["p_exp"], s - 1)
                w = (qb + 1) * P
                qh, ql = qT[h % 2]
                kh, kl = kT[h % 2]
                for c0 in range(0, w, HALF):
                    c = slice(c0, min(w, c0 + HALF))
                    o = psum_all[:, (s % 2) * S + c.start:(s % 2) * S + c.stop]
                    pe.matmul(o, qh[:, q], kh[:, c], start=True, stop=False)
                    pe.matmul(o, qh[:, q], kl[:, c], start=False, stop=False)
                    pe.matmul(o, ql[:, q], kh[:, c], start=False, stop=False)
                    pe.matmul(o, qrA[h % 2][:, q], kA[:, c], start=False, stop=False)
                    last = pe.matmul(o, qrA[h % 2][:, q], kB[:, c], start=False, stop=True)
                last.then_inc(sm["s_mm"], 1)

            def probs_t(s):
                h, qb = divmod(s, TT)
                pe.wait_ge(sm["p_norm"], s + 1)
                for g in range(1 if qb < 4 else 2):
                    tg = tgroup(s, g)
                    if tg >= 2:
                        pe.wait_ge(sm["pt_lo"], tg - 1)
                    for kb in range(4 * g, min(qb + 1, 4 * g + 4)):
                        last = pe.transpose(psum[4 + tg % 2][:, (kb - 4 * g) * P:(kb - 4 * g + 1) * P],
                                            p_sb[s % 2][:, kb * P:(kb + 1) * P], ident[:, :])
                    last.then_inc(sm["t_mm"], 1)

            def values(s):
                h, qb = divmod(s, TT)
                sb = qb // 4
                pe.wait_ge(sm["pt_lo"], tgroup(s, 0 if qb < 4 else 1) + 1)
                n = 2 * h + sb
                if n >= 1:
                    pe.wait_ge(sm["om_ev"], n)
                vh, vl = vv[h % 2]
                for kb in range(4 * sb + 4):
                    c = slice(max(0, kb - 4 * sb) * P, HALF)
                    pe.matmul(psum[6][:, c], vh[:, kb, :], pT_hi[:, kb, c], start=kb == 0, stop=False)
                    pe.matmul(psum[6][:, c], vh[:, kb, :], pT_lo[:, kb, c], start=False, stop=False)
                    last = pe.matmul(psum[6][:, c], vl[:, kb, :], pT_hi[:, kb, c], start=False, stop=kb == 4 * sb + 3)
                last.then_inc(sm["pv_mm"], 1)

            pe.wait_ge(*ev_at[-1])
            pe.wait_ge(*ev_at[-3])
            for j in range(6):
                project(0, j)
            for s in range(STEPS + 3):
                h, qb = divmod(s, TT)
                if s < STEPS:
                    scores(s)
                if s >= 3 and (s - 3) % 4 == 3:
                    values(s - 3)
                if 2 <= s < STEPS + 2:
                    probs_t(s - 2)
                if h + 1 < MH and qb < 6:
                    project(h + 1, qb)

            pe.wait_ge(sm["ad2"], KT)
            for j in range(4):
                n = need(("mlao", j))
                for jj in range(4):
                    g = 4 * j + jj
                    if g >= 4:
                        pe.wait_ge(sm["mo_ev"], g - 3)
                    split3(psum[g % 4], [(w_part(n, k, jj // 2 * P, P), w_part(n, k, jj // 2 * P, P, True),
                                          mT_hi[:, k, jj % 2 * HALF:(jj % 2 + 1) * HALF], mT_lo[:, k, jj % 2 * HALF:(jj % 2 + 1) * HALF])
                                         for k in range(KT)]).then_inc(sm["mo_mm"], 1)
            pe.wait_ge(sm["mix_lo"], 16)
            for dh in range(2):
                for part in range(2):
                    n = need(("wout", 2 * dh + part))
                    for t in range(TT):
                        if dh == 1 and part == 0:
                            pe.wait_ge(sm["wo_ev"], t + 1)
                        last = split3(psum[t], [(xm_hi[:, 4 * part + k, t * P:(t + 1) * P], xm_lo[:, 4 * part + k, t * P:(t + 1) * P],
                                                 w_part(n, k, 0, HALF), w_part(n, k, 0, HALF, True)) for k in range(4)],
                                      start=part == 0, stop=part == 1)
                        if part == 1:
                            last.then_inc(sm["wo_mm"], 1)
                        elif t == TT - 1:
                            last.then_inc(w_used, 1)
            for t in range(TT):
                pe.wait_ge(sm["ln_ok"], t + 1)
                for g in range(2):
                    i = 2 * t + g
                    if i >= 4:
                        pe.wait_ge(sm["hT_lo"], i - 3)
                    else:
                        pe.wait_ge(sm["wo_ev"], TT + i + 1)
                    for j in range(4):
                        last = pe.transpose(psum[i % 4][:, j * P:(j + 1) * P], h_tok[:, t, (4 * g + j) * P:(4 * g + j + 1) * P], ident[:, :])
                    last.then_inc(sm["hT_mm"], 1)
            pe.wait_ge(sm["hT_lo"], 2 * TT)
            for i in range(FT):
                n = need(("up", i))
                if i >= 2:
                    pe.wait_ge(sm["up_c"], 4 * (i - 1))
                for g in range(4):
                    split3(psum[4 * (i % 2) + g], [(w_part(n, k, g // 2 * P, P), w_part(n, k, g // 2 * P, P, True),
                                                    hT_hi[:, k, g % 2 * HALF:(g % 2 + 1) * HALF], hT_lo[:, k, g % 2 * HALF:(g % 2 + 1) * HALF])
                                                   for k in range(KT)]).then_inc(sm["up_mm"], 1)
            pe.wait_ge(sm["up_c"], 4 * FT)
            for i in range(FT):
                dh, kk = divmod(i, FT // 2)
                n = need(("down", i))
                pe.wait_ge(sm["fs_lo"], i + 1)
                for t in range(TT):
                    if dh == 1 and kk == 0:
                        pe.wait_ge(sm["dn_ev"], t + 1)
                    last = split3(psum[t], [(f_hi[i % 2][:, k, t * P:(t + 1) * P], f_lo[i % 2][:, k, t * P:(t + 1) * P],
                                             w_part(n, k, 0, HALF), w_part(n, k, 0, HALF, True)) for k in range(2)],
                                  start=kk == 0, stop=kk == FT // 2 - 1)
                    if kk == FT // 2 - 1:
                        last.then_inc(sm["dn_mm"], 1)
                    elif t == TT - 1:
                        last.then_inc(w_used, 1)

        @block.vector
        def _(ve):
            vc = Chain(ve, vs)

            def op(ins):
                vc.done(ins)
                vc.wait()

            def split_lo(lo, src, hi, s_=None):
                return nc.vector.tensor_tensor(lo, src, hi.bitcast(F32), ALU.subtract)

            V = nc.vector
            ve.wait_ge(consts, 11)
            for t in range(TT):
                for g in range(2):
                    i = 2 * t + g
                    ve.wait_ge(xt_hi, i + 1)
                    c = slice(t * P, (t + 1) * P)
                    split_lo(xT_lo[:, 4 * g:4 * g + 4, c], psum[i % 4].rearrange("p (a b) -> p a b", a=4),
                             xT_hi[:, 4 * g:4 * g + 4, c]).then_inc(xt_lo, 1)
            ve.wait_ge(sm["par_mm"], 1)
            V.tensor_copy(cw[:, :, :], psum[7][:, 0:8 * FT].rearrange("p (a b) -> p a b", a=4)).then_inc(sm["par_ok"], 1)

            n_sig = [0]

            def og_group(h, j):
                vt, half = divmod(j, 2)
                n_sig[0] += 1
                ve.wait_ge(sm["sig_ok"], n_sig[0])
                V.scalar_tensor_tensor(og_s[h % 2][:, vt, half * HALF:(half + 1) * HALF], bank(("og", h, j)), norm_g[:, vt:vt + 1],
                                       sig[(n_sig[0] - 1) % 2][:, :], ALU.mult, ALU.mult).then_inc(ev_v, 1)

            def gate_sums(h):
                ve.wait_ge(sm["gate_l"], h + 1)
                op(V.scalar_tensor_tensor(gb_n[:, :], gb_b[:, :], 0.0, gb_e[:, :], ALU.min, ALU.subtract))
                for c in range(CHUNKS):
                    cc = slice(c * CHUNK, (c + 1) * CHUNK)
                    vc.done(V.tensor_tensor_scan(gb_b[:, cc], ones64[:, :], gb_n[:, cc], 0.0, ALU.mult, ALU.add))
                vc.wait()
                b3 = gb_b[:, :].rearrange("p (c i) -> p c i", i=CHUNK)
                n3 = gb_n[:, :].rearrange("p (c i) -> p c i", i=CHUNK)
                op(V.tensor_copy(b_last[:, :], b3[:, :, CHUNK - 1]))
                V.tensor_tensor(n3, b_last[:, :].unsqueeze(2).broadcast_to((P, CHUNKS, CHUNK)), b3, ALU.subtract).then_inc(sm["gate_scan"], 1)

            def prep(h):
                ve.wait_ge(sm["gate_exp"], h + 1)
                ve.wait_ge(*ev_at[gid[("qk", h, 3)]])
                op(V.scalar_tensor_tensor(q_raw[:, :], q_raw[:, :], DK ** -0.5, gb_e[:, :], ALU.mult, ALU.mult))
                vc.done(V.tensor_tensor(k_in[:, :], k_raw[:, :], gb_b[:, :], ALU.mult))
                vc.wait()
                op(V.tensor_tensor(k_raw[:, :], k_raw[:, :], gb_n[:, :], ALU.mult))
                q4v = q_raw[:, :].rearrange("p (t c i) -> p t c i", c=2, i=CHUNK)
                x4v = q_x[:, :].rearrange("p (t c i) -> p t c i", c=2, i=CHUNK)
                k4v = k_raw[:, :].rearrange("p (t c i) -> p t c i", c=2, i=CHUNK)
                u4v = k_up[:, :].rearrange("p (t c i) -> p t c i", c=2, i=CHUNK)
                d2 = dec[:, :].rearrange("p (t c) -> p t c", c=2)
                vc.done(V.tensor_copy(x4v[:, :, 0, :], q4v[:, :, 0, :]))
                vc.done(V.tensor_tensor(x4v[:, :, 1, :], q4v[:, :, 1, :], d2[:, :, 0].unsqueeze(2).broadcast_to((P, TT, CHUNK)), ALU.mult))
                vc.done(V.tensor_copy(u4v[:, :, 1, :], k4v[:, :, 1, :]))
                vc.done(V.tensor_tensor(u4v[:, :, 0, :], k4v[:, :, 0, :], d2[:, :, 1].unsqueeze(2).broadcast_to((P, TT, CHUNK)), ALU.mult))
                V.tensor_tensor(dec2[:, :], d2[:, :, 0], d2[:, :, 1], ALU.mult).then_inc(sm["prep_done"], 1)

            def att_mask(h, t):
                i = h * TT + t
                ve.wait_ge(sm["att_mm"], i + 1)
                if i >= 2:
                    ve.wait_ge(sm["ou_mm"], i - 1)
                a = att[i % 2]
                op(V.tensor_scalar(a[:, :], psum[4][:, 0:P], 3.0e38, -3.0e38, ALU.min, ALU.max))
                op(V.tensor_tensor(a[:, :], a[:, :], mask_gla[:, :], ALU.mult))
                V.tensor_copy(a[0:CHUNK, CHUNK:P], psum[4][0:CHUNK, P:P + CHUNK]).then_inc(sm["att_ok"], 1)

            def state_up(h, t):
                i = h * TT + t
                ve.wait_ge(sm["ou_mm"], i + 1)
                if t == 0:
                    V.tensor_copy(state[:, :], psum[6][:, 0:DV]).then_inc(sm["st_ev"], 1)
                else:
                    ve.wait_ge(sm["st_ev"], i)
                    V.scalar_tensor_tensor(state[:, :], state[:, :], dec2[:, t:t + 1], psum[6][:, 0:DV], ALU.mult, ALU.add).then_inc(sm["st_ev"], 1)

            for j in range(4):
                og_group(0, j)
            gate_sums(0)
            prep(0)
            for h in range(GH):
                for t in range(TT):
                    att_mask(h, t)
                    if h < GH - 1 and t < 4:
                        og_group(h + 1, t)
                    state_up(h, t)
                ve.wait_ge(sm["o_ev"], TT * (h + 1))
                V.tensor_scalar(rs, ss, 1.0 / DV, RMS_EPS, ALU.mult, ALU.add).then_inc(sm["norm_v"], 1)
                ve.wait_ge(sm["norm_s"], h + 1)
                op(V.reciprocal(rs, rs))
                V.tensor_tensor(o_tok[:, :, :], o_tok[:, :, :], rs.unsqueeze(2).broadcast_to((P, TT, DV)), ALU.mult).then_inc(sm["o_scaled"], 1)
                if h < GH - 1:
                    gate_sums(h + 1)
                for j in range(4):
                    vt, half = divmod(j, 2)
                    u = 4 * h + j
                    kind = ("oT", h, j)
                    ve.wait_ge(mm, gid[kind] + 1)
                    if u >= 2:
                        ve.wait_ge(oT_out[u % 2], 16 * (u // 2))
                    V.tensor_tensor(oT_st[u % 2][:, :], bank(kind), og_s[h % 2][:, vt, half * HALF:(half + 1) * HALF], ALU.mult).then_inc(ev_v, 1)
                if h < GH - 1:
                    prep(h + 1)

            for k in range(KT):
                ve.wait_ge(sm["op_hi"], k + 1)
                split_lo(oT_lo[:, k, :], ld_st[k % 2][:, :], oT_hi[:, k, :]).then_inc(sm["op_lo"], 1)
            for g in range(16):
                j, jj = divmod(g, 4)
                kind = ("glao", j, jj)
                ve.wait_ge(mm, gid[kind] + 1)
                ve.wait_ge(ga_in[g % 2], 16 * (g // 2 + 1))
                if g >= 2:
                    ve.wait_ge(m_out[g % 2], 16 * (g // 2))
                V.tensor_tensor(m_st[g % 2][:, :], bank(kind), ga_st[g % 2][:, :], ALU.mult).then_inc(ev_v, 1)

            MAGIC = 12582912.0
            C1 = 6.28125
            C2 = 0.0019350051879882812
            C3 = 2 * PI - C1 - C2
            ve.wait_ge(m_out[0], 16 * 8)
            ve.wait_ge(m_out[1], 16 * 8)
            ve.wait_ge(sm["ad2"], 0) if False else None
            for i in range(HR):
                vc.done(V.memset(ifreq[:, i:i + 1], THETA ** (-i / HR)))
            ve.wait_ge(sm["pos_ok"], 16)
            op(V.tensor_copy(rs, pos_i[:, :]))
            f3 = (P, TT, HR)
            op(V.tensor_tensor(rtmp[:, :, :], rs.unsqueeze(2).broadcast_to(f3), ifreq[:, :].unsqueeze(1).broadcast_to(f3), ALU.mult))
            for tab, quarter in ((sin, 0.0), (cos, 0.25)):
                op(V.tensor_scalar(rtmp2[:, :, :], rtmp[:, :, :], 1.0 / (2 * PI), quarter, ALU.mult, ALU.add))
                op(V.tensor_scalar(rtmp2[:, :, :], rtmp2[:, :, :], MAGIC, None, ALU.add))
                op(V.tensor_scalar(rtmp2[:, :, :], rtmp2[:, :, :], MAGIC, None, ALU.subtract))
                op(V.scalar_tensor_tensor(tab[:, :, :], rtmp2[:, :, :], -C1, rtmp[:, :, :], ALU.mult, ALU.add))
                op(V.scalar_tensor_tensor(tab[:, :, :], rtmp2[:, :, :], -C2, tab[:, :, :], ALU.mult, ALU.add))
                op(V.scalar_tensor_tensor(tab[:, :, :], rtmp2[:, :, :], -C3, tab[:, :, :], ALU.mult, ALU.add))
                if quarter:
                    op(V.tensor_scalar(tab[:, :, :], tab[:, :, :], PI / 2, None, ALU.add))
                V.tensor_scalar(tab[:, :, :], tab[:, :, :], 3.1415925, -3.1415925, ALU.min, ALU.max).then_inc(sm["angs"], 1)

            ve.wait_ge(sm["lat_sq"], 2 * TT)
            rq, rk = small[:, 16:24], small[:, 24:32]
            vc.done(V.tensor_scalar(rq, rq, 1.0 / QR, RMS_EPS, ALU.mult, ALU.add))
            V.tensor_scalar(rk, rk, 1.0 / KR, RMS_EPS, ALU.mult, ALU.add).then_inc(sm["lat_v"], 1)
            ve.wait_ge(sm["lat_s"], 1)
            op(V.reciprocal(small[:, 16:32], small[:, 16:32]))
            vc.done(V.tensor_tensor(c_tok[:, :, 0:QR], c_tok[:, :, 0:QR], rq.unsqueeze(2).broadcast_to((P, TT, QR)), ALU.mult))
            V.tensor_tensor(c_tok[:, :, QR:QR + KR], c_tok[:, :, QR:QR + KR], rk.unsqueeze(2).broadcast_to((P, TT, KR)), ALU.mult).then_inc(sm["lat_ok"], 1)

            def rotate(x1, x2, cs, sn, r1, r2, t1, t2, last_read):
                vc.done(V.tensor_tensor(t1, x1, cs, ALU.mult))
                vc.done(V.tensor_tensor(t2, x2, sn, ALU.mult))
                vc.wait()
                op(V.tensor_tensor(r1, t1, t2, ALU.subtract))
                vc.done(V.tensor_tensor(t1, x2, cs, ALU.mult))
                last_read(V.tensor_tensor(t2, x1, sn, ALU.mult))
                op(V.tensor_tensor(r2, t1, t2, ALU.add))

            ve.wait_ge(sm["sins"], 2)
            kr0 = QR + KR
            rot = c_tok[:, :, kr0:kr0 + ROPE]

            def chain_read(ins):
                vc.done(ins)
                vc.wait()

            rotate(c_tok[:, :, kr0:kr0 + HR], c_tok[:, :, kr0 + HR:kr0 + ROPE], cos[:, :, :], sin[:, :, :],
                   kst3[:, :, 0:HR], kst3[:, :, HR:ROPE], rtmp[:, :, :], rtmp2[:, :, :], chain_read)
            op(V.tensor_copy(rot, kst3[:, :, 0:ROPE]))
            op(V.tensor_copy(kst3[:, :, 0:ROPE].bitcast(F32R), rot))
            vc.done(V.tensor_tensor(kst3[:, :, ROPE:2 * ROPE].bitcast(F32R), rot, kst3[:, :, 0:ROPE], ALU.subtract))
            V.tensor_copy(kst3[:, :, 2 * ROPE:3 * ROPE], kst3[:, :, 0:ROPE]).then_inc(sm["kst3_ok"], 1)
            for c in range(QKT + KVT):
                for half in range(2):
                    hs = slice(half * HALF, (half + 1) * HALF)
                    ve.wait_ge(sm["hi_ok"], 2 * c + half + 1)
                    V.scalar_tensor_tensor(cT_lo[:, c, hs], bank(("cT", c, half)), lat_g[:, c:c + 1], cT_hi[:, c, hs].bitcast(F32),
                                           ALU.mult, ALU.subtract).then_inc(ev_v, 1)
            h3 = (P, MH, HR)
            for t in range(TT):
                ve.wait_ge(mm, gid[("qr", t)] + 1)
                if t >= 2:
                    ve.wait_ge(mm, gid[("qrT", t - 2, 1)] + 1)
                b3 = bank(("qr", t)).rearrange("p (h c) -> p h c", h=MH)
                R_ = qr_rot[t % 2]

                def bank_read(ins):
                    ins.then_inc(ev_v, 1)
                    ve.wait_ge(*ev_at[gid[("qr", t)]])

                rotate(b3[:, :, 0:HR], b3[:, :, HR:ROPE], cos[:, t, :].unsqueeze(1).broadcast_to(h3), sin[:, t, :].unsqueeze(1).broadcast_to(h3),
                       R_[:, :, 0:HR], R_[:, :, HR:ROPE], qr_tmp[:, :, :], qr_tmp2[:, :, :], bank_read)
                op(V.tensor_copy(qr_hl[t % 2][:, :, 0:ROPE].bitcast(F32R), R_[:, :, :]))
                V.tensor_tensor(qr_hl[t % 2][:, :, ROPE:2 * ROPE].bitcast(F32R), R_[:, :, :], qr_hl[t % 2][:, :, 0:ROPE], ALU.subtract).then_inc(sm["rot_ok"], 1)

            def pj_low(h, j):
                ve.wait_ge(sm["pj_hi"], 6 * h + j + 1)
                kind, half = divmod(j, 2)
                dst = (qT, kT, vv)[kind][h % 2]
                if kind < 2:
                    hs = slice(half * HALF, (half + 1) * HALF)
                    split_lo(dst[1][:, hs], psum[7], dst[0][:, hs]).then_inc(sm["pj_lo"], 1)
                else:
                    ts = slice(4 * half, 4 * half + 4)
                    split_lo(dst[1][:, ts, :], psum[7].rearrange("p (a b) -> p a b", a=4), dst[0][:, ts, :]).then_inc(sm["pj_lo"], 1)

            for j in range(6):
                pj_low(0, j)
            for s in range(STEPS + 2):
                h, qb = divmod(s, TT)
                w = (qb + 1) * P
                b0 = (s % 2) * S
                if s < STEPS:
                    ve.wait_ge(sm["s_mm"], s + 1)
                    d = psum_all[:, b0 + w - P:b0 + w]
                    op(V.tensor_tensor(d, d, mask_att[:, :], ALU.add))
                    op(V.tensor_reduce(nmax[:, s % 2:s % 2 + 1], psum_all[:, b0:b0 + w], AX, ALU.max))
                    if s >= 2:
                        ve.wait_ge(sm["p_exp"], s - 1)
                    V.tensor_scalar(nbias[:, s % 2:s % 2 + 1], nmax[:, s % 2:s % 2 + 1], -ATT_SCALE, None, ALU.mult).then_inc(sm["nb_ok"], 1)
                if 1 <= s <= STEPS:
                    p = s - 1
                    wp = (p % TT + 1) * P
                    ve.wait_ge(sm["p_exp"], p + 1)
                    op(V.reciprocal(prec[:, p % 2:p % 2 + 1], psums[:, p % 2:p % 2 + 1]))
                    V.tensor_scalar(p_sb[p % 2][:, 0:wp], p_sb[p % 2][:, 0:wp], prec[:, p % 2:p % 2 + 1], None, ALU.mult).then_inc(sm["p_norm"], 1)
                if s >= 2:
                    p = s - 2
                    pq = p % TT
                    for g in range(1 if pq < 4 else 2):
                        tg = tgroup(p, g)
                        n = min(pq + 1 - 4 * g, 4)
                        ve.wait_ge(sm["pt_hi"], tg + 1)
                        c = slice(pq % 4 * P, (pq % 4 + 1) * P)
                        split_lo(pT_lo[:, 4 * g:4 * g + n, c], psum[4 + tg % 2][:, 0:n * P].rearrange("p (a b) -> p a b", a=n),
                                 pT_hi[:, 4 * g:4 * g + n, c]).then_inc(sm["pt_lo"], 1)
                if h + 1 < MH and qb < 6:
                    pj_low(h + 1, qb)

            for k in range(KT):
                ve.wait_ge(sm["vd2"], k + 1)
                split_lo(mT_lo[:, k, :], ld2[k % 2][:, :], mT_hi[:, k, :]).then_inc(sm["ad2"], 1)
            for g in range(17):
                if g < 16:
                    ve.wait_ge(sm["mo_mm"], g + 1)
                    ve.wait_ge(mx_in[g % 2], 32 * (g // 2 + 1))
                    if g >= 2:
                        ve.wait_ge(sm["mix_lo"], g - 1)
                    V.tensor_tensor(mx[g % 2][:, :], psum[g % 4], sgb_st[g % 2][:, :], ALU.mult).then_inc(sm["mo_ev"], 1)
                    ve.wait_ge(sm["mo_ev"], g + 1)
                    V.tensor_tensor(mx[g % 2][:, :], mx[g % 2][:, :], mm_st[g % 2][:, :], ALU.add).then_inc(sm["mix_ok"], 1)
                if g >= 1:
                    f, hs = (g - 1) // 2, slice((g - 1) % 2 * HALF, ((g - 1) % 2 + 1) * HALF)
                    ve.wait_ge(sm["mix_hi"], g)
                    split_lo(xm_lo[:, f, hs], mx[(g - 1) % 2][:, :], xm_hi[:, f, hs]).then_inc(sm["mix_lo"], 1)

            def norm_rows(rows, stats, mvt, rst, t, sem_v, sem_s, gain, bias, ok):
                vc.done(V.bn_stats(stats[:, t, 0:6], rows[:, t, 0:HALF]))
                vc.done(V.bn_stats(stats[:, t, 6:12], rows[:, t, HALF:D]))
                vc.wait()
                op(V.bn_aggr(mvt[:, t, :], stats[:, t, :]))
                V.tensor_scalar(rst[:, t, 0:1], mvt[:, t, 1:2], LN_EPS, None, ALU.add).then_inc(sem_v, 1)
                ve.wait_ge(sem_s, t + 1)
                op(V.reciprocal(rst[:, t, 1:2], rst[:, t, 0:1]))
                op(V.tensor_scalar(rows[:, t, :], rows[:, t, :], mvt[:, t, 0:1], rst[:, t, 1:2], ALU.subtract, ALU.mult))
                op(V.tensor_tensor(rows[:, t, :], rows[:, t, :], gain[:, :], ALU.mult))
                V.tensor_tensor(rows[:, t, :], rows[:, t, :], bias[:, :], ALU.add).then_inc(ok, 1)

            ve.wait_ge(ln1_in, 32)
            for dh in range(2):
                for t in range(TT):
                    c = slice(dh * HALF, (dh + 1) * HALF)
                    ve.wait_ge(row_in[t], 16)
                    ve.wait_ge(sm["wo_mm"], dh * TT + t + 1)
                    V.scalar_tensor_tensor(h_tok[:, t, c], h_tok[:, t, c], ALPHA, psum[t], ALU.mult, ALU.add).then_inc(sm["wo_ev"], 1)
                    if dh == 1:
                        ve.wait_ge(sm["wo_ev"], TT + t + 1)
                        norm_rows(h_tok, bst, mv, lrs, t, sm["ln_v"], sm["ln_s"], ln_g, ln_b, sm["ln_ok"])
            for i in range(2 * TT):
                t, g = divmod(i, 2)
                c = slice(t * P, (t + 1) * P)
                ve.wait_ge(sm["hT_hi"], i + 1)
                split_lo(hT_lo[:, 4 * g:4 * g + 4, c], psum[i % 4].rearrange("p (a b) -> p a b", a=4),
                         hT_hi[:, 4 * g:4 * g + 4, c]).then_inc(sm["hT_lo"], 1)

            def conv(dst, b0, half, fcol, done):
                c0 = half * HALF
                lo = 1 if half == 0 else 0
                op(V.scalar_tensor_tensor(dst[:, lo:HALF], psum_all[:, b0 + c0 + lo - 1:b0 + c0 + HALF - 1], cw[:, 1, fcol:fcol + 1],
                                          dst[:, lo:HALF], ALU.mult, ALU.add))
                lo = 2 if half == 0 else 0
                V.scalar_tensor_tensor(dst[:, lo:HALF], psum_all[:, b0 + c0 + lo - 2:b0 + c0 + HALF - 2], cw[:, 0, fcol:fcol + 1],
                                       dst[:, lo:HALF], ALU.mult, ALU.add).then_inc(sm["up_c"], 1)

            for i in range(FT):
                b0 = 4 * (i % 2) * HALF
                for half in range(2):
                    n = 2 * i + half
                    ve.wait_ge(sm["up_a"], 2 * n + 1)
                    conv(up_g, b0, half, i, None)
                    ve.wait_ge(sm["up_a"], 2 * n + 2)
                    conv(up_v, b0 + 2 * HALF, half, FT + i, None)
                    ve.wait_ge(sm["up_c"], 2 * n + 2)
                    ve.wait_ge(sm["up_si"], n + 1)
                    V.tensor_tensor(f_all[:, i, half * HALF:(half + 1) * HALF], up_g[:, :], up_v[:, :], ALU.mult).then_inc(sm["up_f"], 1)

            ve.wait_ge(sm["up_mm"], 4 * FT)
            for dh in range(2):
                for kk in range(FT // 2):
                    i = dh * (FT // 2) + kk
                    ve.wait_ge(sm["fs_hi"], i + 1)
                    split_lo(f_lo[i % 2][:, :, :], f_all[:, 2 * kk:2 * kk + 2, :], f_hi[i % 2][:, :, :]).then_inc(sm["fs_lo"], 1)
                    if dh == 1 and kk == 0:
                        for t in range(TT):
                            ve.wait_ge(row2_in[t], 16)
                            ve.wait_ge(sm["dn_mm"], t + 1)
                            V.scalar_tensor_tensor(z_tok[:, t, 0:HALF], z_tok[:, t, 0:HALF], ALPHA, psum[t], ALU.mult, ALU.add).then_inc(sm["dn_ev"], 1)
            ve.wait_ge(ln2_in, 32)
            for t in range(TT):
                ve.wait_ge(sm["dn_mm"], TT + t + 1)
                V.scalar_tensor_tensor(z_tok[:, t, HALF:D], z_tok[:, t, HALF:D], ALPHA, psum[t], ALU.mult, ALU.add).then_inc(sm["dn_ev"], 1)
                ve.wait_ge(sm["dn_ev"], TT + t + 1)
                norm_rows(z_tok, bst2, mv2, lrs2, t, sm["ln2_v"], sm["ln2_s"], ln2_gt, ln2_bt, sm["ln2_ok"])

        @block.scalar
        def _(ac):
            A = nc.scalar
            sc = Chain(ac, as_)

            def op(ins):
                sc.done(ins)
                sc.wait()

            for k in range(3):
                ac.dma_start(cw_rows[:, k, :], conv_w[0, k].rearrange("(j p) -> j p", p=P)).then_inc(par_landed, 16)
            ac.dma_start(cw_rows[:, 3, :], conv_b[0].rearrange("(j p) -> j p", p=P)).then_inc(par_landed, 16)
            ac.dma_start(w_gate[:, :], gla_w_gate_up[0]).then_inc(par_landed, 16)
            with nc.allow_non_contiguous_dma("a few hundred parameters, once"):
                ac.dma_start(b_gate[:, :], gla_b_gate[0].rearrange("(j p) -> p j", p=P)).then_inc(par_landed, 16)
                ac.dma_start(norm_g[:, :], gla_norm_g[0].rearrange("(j p) -> p j", p=P)).then_inc(par_landed, 16)
                ac.dma_start(lat_g[:, 0:QKT], mla_q_norm_g[0].rearrange("(j p) -> p j", p=P)).then_inc(par_landed, 16)
                ac.dma_start(lat_g[:, QKT:], mla_kv_norm_g[0].rearrange("(j p) -> p j", p=P)).then_inc(par_landed, 16)
            for i in range(2 * TT):
                t, g = divmod(i, 2)
                ac.wait_ge(xt_done, i + 1)
                A.copy(xT_hi[:, 4 * g:4 * g + 4, t * P:(t + 1) * P], psum[i % 4].rearrange("p (a b) -> p a b", a=4)).then_inc(xt_hi, 1)
            ac.wait_ge(par_landed, 16 * PARAMS)

            sig_users = []
            stored = [0, 0]

            def stage():
                u = len(sig_users)
                if u >= 2:
                    ac.wait_ge(*sig_users[u - 2])
                return u

            def got(kind):
                ac.wait_ge(mm, gid[kind] + 1)
                return bank(kind)

            def og_group(h, j):
                u = stage()
                b = got(("og", h, j))
                A.activation(sig[u % 2][:, :], b, ACT.Sigmoid).then_inc(sm["sig_ok"], 1)
                sig_users.append(ev_at[gid[("og", h, j)]])

            def gate_group(kind, dst):
                name, c, j = kind
                u = stage()
                b = got(kind)
                A.activation(sig[u % 2][:, :], b, ACT.Sigmoid).then_inc(ev_a, 1)
                ac.wait_ge(*ev_at[gid[kind]])
                f = 2 * c + j // 2
                stored[u % 2] += 16
                ac.dma_start(dst[f * P:(f + 1) * P, j % 2 * HALF:(j % 2 + 1) * HALF], sig[u % 2][:, :]).then_inc(sig_st[u % 2], 16)
                sig_users.append((sig_st[u % 2], stored[u % 2]))

            def v_group(h, j):
                A.copy(v_tok[h % 2][:, 2 * j:2 * j + 2, :], got(("v", h, j)).rearrange("p (a b) -> p a b", a=2)).then_inc(ev_a, 1)

            def gates(h):
                ac.wait_ge(sm["gate_mm"], h + 1)
                if h >= 1:
                    ac.wait_ge(sm["prep_done"], h)
                for half in range(2):
                    hs = slice(half * HALF, (half + 1) * HALF)
                    sc.done(A.activation(gb_b[:, hs], psum[4 + half], ACT.Identity, bias=b_gate[:, h:h + 1]))
                    sc.done(A.activation(gb_e[:, hs], psum[4 + half], ACT.Abs, bias=b_gate[:, h:h + 1]))
                sc.wait()
                op(A.activation(gb_e[:, :], gb_e[:, :], ACT.Exp, scale=-1.0))
                A.activation(gb_e[:, :], gb_e[:, :], ACT.Ln, bias=1.0).then_inc(sm["gate_l"], 1)
                ac.wait_ge(sm["gate_scan"], h + 1)
                sc.done(A.activation(gb_e[:, :], gb_b[:, :], ACT.Exp, scale=1.0 / TAU))
                sc.done(A.activation(gb_n[:, :], gb_n[:, :], ACT.Exp, scale=1.0 / TAU))
                sc.done(A.activation(dec[:, :], b_last[:, :], ACT.Exp, scale=1.0 / TAU))
                A.activation(gb_b[:, :], gb_b[:, :], ACT.Exp, scale=-1.0 / TAU).then_inc(sm["gate_exp"], 1)

            def qk_groups(h):
                for j in range(4):
                    dst, hs = (q_raw, k_raw)[j // 2], slice(j % 2 * HALF, (j % 2 + 1) * HALF)
                    A.copy(dst[:, hs], got(("qk", h, j))).then_inc(ev_a, 1)

            for half in range(2):
                A.copy(rT[:, half * HALF:(half + 1) * HALF], got(("r", half))[0:RANK, :]).then_inc(ev_a, 1)
            for j in range(4):
                og_group(0, j)
            for j in range(4):
                v_group(0, j)
            gates(0)
            qk_groups(0)
            for h in range(GH):
                last_head = h == GH - 1
                for t in range(TT):
                    i = h * TT + t
                    ac.wait_ge(sm["att_mm"], i + 1)
                    if i >= 2:
                        ac.wait_ge(sm["ou_mm"], i - 1)
                    A.copy(kst[i % 2][:, :], psum[7][:, 0:P]).then_inc(sm["kst_ok"], 1)
                    if last_head:
                        gate_group(("ga", t // 4, t % 4), d_sga)
                    elif t < 4:
                        og_group(h + 1, t)
                    else:
                        v_group(h + 1, t - 4)
                    ac.wait_ge(sm["ou_mm"], i + 1)
                    sc.done(A.copy(o_tok[:, t, :], psum[5][:, 0:DV]))
                    sc.wait()
                    A.activation(sq_junk[:, :], o_tok[:, t, :], ACT.Square, accum_out=small[:, t:t + 1]).then_inc(sm["o_ev"], 1)
                ac.wait_ge(sm["norm_v"], h + 1)
                A.activation(rs, rs, ACT.Sqrt).then_inc(sm["norm_s"], 1)
                if not last_head:
                    gates(h + 1)
                    qk_groups(h + 1)
                for j in range(4):
                    u = 4 * h + j
                    vt, half = divmod(j, 2)
                    ac.wait_ge(*ev_at[gid[("oT", h, j)]])
                    row = h * DV + vt * P
                    ac.dma_start(d_og[row:row + P, half * HALF:(half + 1) * HALF], oT_st[u % 2][:, :]).then_inc(oT_out[u % 2], 16)
                if not last_head:
                    for j in range(4):
                        gate_group(("gb", h, j), d_sgb)
            ac.wait_ge(oT_out[0], 16 * 8)
            ac.wait_ge(oT_out[1], 16 * 8)
            ac.wait_ge(sm["o_scaled"], GH)

            def op_load(k):
                ac.dma_start(ld_st[k % 2][:, :], d_og[k * P:(k + 1) * P, :]).then_inc(ld_in[k % 2], 16)

            for j in range(8):
                gate_group(("ga", 2 + j // 4, j % 4), d_sga)
            ac.wait_ge(sig_st[0], stored[0])
            ac.wait_ge(sig_st[1], stored[1])
            op_load(0)
            op_load(1)
            for k in range(KT):
                ac.wait_ge(ld_in[k % 2], 16 * (k // 2 + 1))
                A.copy(oT_hi[:, k, :], ld_st[k % 2][:, :]).then_inc(sm["op_hi"], 1)
                if k + 2 < KT:
                    ac.wait_ge(sm["op_lo"], k + 1)
                    op_load(k + 2)

            def ga_load(g):
                f, half = divmod(g, 2)
                ac.dma_start(ga_st[g % 2][:, :], d_sga[f * P:(f + 1) * P, half * HALF:(half + 1) * HALF]).then_inc(ga_in[g % 2], 16)

            ga_load(0)
            ga_load(1)
            for g in range(16):
                f, half = divmod(g, 2)
                kind = ("glao", g // 4, g % 4)
                ac.wait_ge(*ev_at[gid[kind]])
                ac.dma_start(d_m[f * P:(f + 1) * P, half * HALF:(half + 1) * HALF], m_st[g % 2][:, :]).then_inc(m_out[g % 2], 16)
                if g + 2 < 16:
                    ga_load(g + 2)
            ac.wait_ge(m_out[0], 16 * 8)
            ac.wait_ge(m_out[1], 16 * 8)
            with nc.allow_non_contiguous_dma("1024 positions, once"):
                ac.dma_start(pos_i[:, :], positions[0].rearrange("(t p) -> p t", p=P)).then_inc(sm["pos_ok"], 16)
            for j, (c0, c) in enumerate(LAT):
                for t in range(TT):
                    A.copy(c_tok[:, t, c0:c0 + c], got(("lat", j, t))[:, 0:c]).then_inc(ev_a, 1)
            ac.wait_ge(*ev_at[gid[("lat", 2, TT - 1)]])
            for t in range(TT):
                if t:
                    ac.wait_ge(sm["lat_sq"], 2 * t)
                A.activation(junk2[:, :], c_tok[:, t, 0:QR], ACT.Square, accum_out=small[:, 16 + t:17 + t]).then_inc(sm["lat_sq"], 1)
                ac.wait_ge(sm["lat_sq"], 2 * t + 1)
                A.activation(junk2[:, 0:KR], c_tok[:, t, QR:QR + KR], ACT.Square, accum_out=small[:, 24 + t:25 + t]).then_inc(sm["lat_sq"], 1)
            ac.wait_ge(sm["lat_v"], 1)
            A.activation(small[:, 16:32], small[:, 16:32], ACT.Sqrt).then_inc(sm["lat_s"], 1)
            ac.wait_ge(sm["angs"], 2)
            A.activation(sin[:, :, :], sin[:, :, :], ACT.Sin).then_inc(sm["sins"], 1)
            A.activation(cos[:, :, :], cos[:, :, :], ACT.Sin).then_inc(sm["sins"], 1)
            gs = [0, 0]
            for j in range(4):
                kind = ("gb", 3, j)
                b = got(kind)
                if j >= 2:
                    ac.wait_ge(sig_st[j % 2], stored[j % 2])
                A.activation(gsig2[j % 2][:, :], b, ACT.Sigmoid).then_inc(ev_a, 1)
                ac.wait_ge(*ev_at[gid[kind]])
                f = 6 + j // 2
                stored[j % 2] += 16
                ac.dma_start(d_sgb[f * P:(f + 1) * P, j % 2 * HALF:(j % 2 + 1) * HALF], gsig2[j % 2][:, :]).then_inc(sig_st[j % 2], 16)
            for c in range(QKT + KVT):
                for half in range(2):
                    A.activation(cT_hi[:, c, half * HALF:(half + 1) * HALF], got(("cT", c, half)), ACT.Copy, scale=lat_g[:, c:c + 1]).then_inc(sm["hi_ok"], 1)
            for m in range(2):
                for half in range(2):
                    A.copy((kA, kB)[m][:, half * HALF:(half + 1) * HALF], got(("kT", m, half))).then_inc(ev_a, 1)
            for t in range(TT):
                for g in range(2):
                    b = got(("qrT", t, g))
                    if g == 0 and t >= 2:
                        ac.wait_ge(qs_out[t % 2], 16 * (t // 2))
                    A.copy(qr_st[t % 2][:, 4 * g:4 * g + 4, :], b.rearrange("p (a b) -> p a b", a=4)).then_inc(ev_a, 1)
                ac.wait_ge(*ev_at[gid[("qrT", t, 1)]])
                ac.dma_start(d_qr.rearrange("h p s -> p h s")[:, :, t * P:(t + 1) * P], qr_st[t % 2][:, :, :]).then_inc(qs_out[t % 2], 16)

            ac.wait_ge(qs_out[0], 16 * 4)
            ac.wait_ge(qs_out[1], 16 * 4)
            ac.wait_ge(sig_st[0], stored[0])
            ac.wait_ge(sig_st[1], stored[1])

            def qr_load(h):
                ac.dma_start(qrA[h % 2][:, :].bitcast(F32), d_qr[h]).then_inc(qrA_in[h % 2], 16)

            qr_load(0)

            def pj_high(h, j):
                ac.wait_ge(sm["pj_mm"], 6 * h + j + 1)
                kind, half = divmod(j, 2)
                dst = (qT, kT, vv)[kind][h % 2]
                if kind < 2:
                    A.copy(dst[0][:, half * HALF:(half + 1) * HALF], psum[7]).then_inc(sm["pj_hi"], 1)
                else:
                    A.copy(dst[0][:, 4 * half:4 * half + 4, :], psum[7].rearrange("p (a b) -> p a b", a=4)).then_inc(sm["pj_hi"], 1)

            for j in range(6):
                pj_high(0, j)
            for s in range(STEPS + 3):
                h, qb = divmod(s, TT)
                if qb == 0 and h + 1 < MH:
                    if h >= 1:
                        ac.wait_ge(sm["s_mm"], TT * h)
                    qr_load(h + 1)
                if s >= 3 and (s - 3) % 4 == 3:
                    n = (s - 3) // 4
                    ac.wait_ge(sm["pv_mm"], n + 1)
                    if n >= 2:
                        ac.wait_ge(om_out[n % 2], 16 * (n // 2))
                    A.copy(om_st[n % 2][:, :], psum[6]).then_inc(sm["om_ev"], 1)
                    ac.wait_ge(sm["om_ev"], n + 1)
                    ac.dma_start(d_om[n // 2 * MV:(n // 2 + 1) * MV, n % 2 * HALF:(n % 2 + 1) * HALF], om_st[n % 2][:, :]).then_inc(om_out[n % 2], 16)
                if 2 <= s < STEPS + 2:
                    p = s - 2
                    pq = p % TT
                    for g in range(1 if pq < 4 else 2):
                        tg = tgroup(p, g)
                        n = min(pq + 1 - 4 * g, 4)
                        ac.wait_ge(sm["t_mm"], tg + 1)
                        A.copy(pT_hi[:, 4 * g:4 * g + n, pq % 4 * P:(pq % 4 + 1) * P], psum[4 + tg % 2][:, 0:n * P].rearrange("p (a b) -> p a b", a=n)).then_inc(sm["pt_hi"], 1)
                if s < STEPS:
                    w = (qb + 1) * P
                    ac.wait_ge(sm["nb_ok"], s + 1)
                    if s >= 2:
                        ac.wait_ge(sm["t_mm"], tgroup(s - 2, 0 if (s - 2) % TT < 4 else 1) + 1)
                        ac.wait_ge(sm["p_norm"], s - 1)
                    A.activation(p_sb[s % 2][:, 0:w], psum_all[:, (s % 2) * S:(s % 2) * S + w], ACT.Exp, bias=nbias[:, s % 2:s % 2 + 1],
                                 scale=ATT_SCALE, accum_out=psums[:, s % 2:s % 2 + 1]).then_inc(sm["p_exp"], 1)
                if h + 1 < MH and qb < 6:
                    pj_high(h + 1, qb)

            ac.wait_ge(om_out[0], 16 * MH)
            ac.wait_ge(om_out[1], 16 * MH)

            def om_load(k):
                ac.dma_start(ld2[k % 2][:, :], d_om[k * P:(k + 1) * P, :]).then_inc(ld_in[k % 2], 16)

            def mix_load(g):
                f, hs = g // 2, slice(g % 2 * HALF, (g % 2 + 1) * HALF)
                ac.dma_start(sgb_st[g % 2][:, :], d_sgb[f * P:(f + 1) * P, hs]).then_inc(mx_in[g % 2], 16)
                ac.dma_start(mm_st[g % 2][:, :], d_m[f * P:(f + 1) * P, hs]).then_inc(mx_in[g % 2], 16)

            om_load(0)
            om_load(1)
            mix_load(0)
            mix_load(1)
            for k in range(KT):
                ac.wait_ge(ld_in[k % 2], 16 * (4 + k // 2 + 1))
                A.copy(mT_hi[:, k, :], ld2[k % 2][:, :]).then_inc(sm["vd2"], 1)
                if k + 2 < KT:
                    ac.wait_ge(sm["ad2"], k + 1)
                    om_load(k + 2)
            for g in range(16):
                ac.wait_ge(sm["mix_ok"], g + 1)
                A.copy(xm_hi[:, g // 2, g % 2 * HALF:(g % 2 + 1) * HALF], mx[g % 2][:, :]).then_inc(sm["mix_hi"], 1)
                if g + 2 < 16:
                    mix_load(g + 2)
            ac.wait_ge(sm["mo_mm"], 16)
            for t in range(TT):
                ac.dma_start(h_tok[:, t, :], x[0, t * P:(t + 1) * P, :]).then_inc(row_in[t], 16)
            ac.dma_start(ln_g[:, :], ln1_g[0].partition_broadcast(P)).then_inc(ln1_in, 16)
            ac.dma_start(ln_b[:, :], ln1_b[0].partition_broadcast(P)).then_inc(ln1_in, 16)
            for t in range(TT):
                ac.wait_ge(sm["ln_v"], t + 1)
                A.activation(lrs[:, t, 0:1], lrs[:, t, 0:1], ACT.Sqrt).then_inc(sm["ln_s"], 1)
            for t in range(TT):
                ac.wait_ge(sm["ln_ok"], t + 1)
                ac.dma_start(d_h[t * P:(t + 1) * P, :], h_tok[:, t, :]).then_inc(sm["h_stored"], 16)
                for g in range(2):
                    i = 2 * t + g
                    ac.wait_ge(sm["hT_mm"], i + 1)
                    A.copy(hT_hi[:, 4 * g:4 * g + 4, t * P:(t + 1) * P], psum[i % 4].rearrange("p (a b) -> p a b", a=4)).then_inc(sm["hT_hi"], 1)
            ac.wait_ge(sm["h_stored"], 16 * TT)
            for i in range(FT):
                for half in range(2):
                    n = 2 * i + half
                    for part, dst in ((0, up_g), (1, up_v)):
                        b = 4 * (i % 2) + 2 * part + half
                        ac.wait_ge(sm["up_mm"], 4 * i + 2 * part + half + 1)
                        if n >= 1:
                            ac.wait_ge(sm["up_f"], n)
                        fc = part * FT + i
                        A.activation(dst[:, :], psum[b], ACT.Identity, bias=cw[:, 3, fc:fc + 1], scale=cw[:, 2, fc:fc + 1]).then_inc(sm["up_a"], 1)
                    ac.wait_ge(sm["up_c"], 2 * n + 1)
                    A.activation(up_g[:, :], up_g[:, :], ACT.Silu).then_inc(sm["up_si"], 1)
            ac.wait_ge(sm["up_f"], 2 * FT)
            ac.wait_ge(sm["up_mm"], 4 * FT)
            for t in range(TT):
                ac.dma_start(z_tok[:, t, :], d_h[t * P:(t + 1) * P, :]).then_inc(row2_in[t], 16)
            for i in range(FT):
                kk = i % (FT // 2)
                if i >= 2:
                    ac.wait_ge(*used_at(slot_no[("down", i - 2)]))
                    ac.wait_ge(sm["fs_lo"], i - 1)
                A.copy(f_hi[i % 2][:, :, :], f_all[:, 2 * kk:2 * kk + 2, :]).then_inc(sm["fs_hi"], 1)
                if i == FT // 2 + 1:
                    ac.wait_ge(sm["fs_lo"], FT // 2 + 1)
                    ac.wait_ge(sm["fs_hi"], FT // 2 + 1)
                    ac.dma_start(ln2_gt[:, :], ln2_g[0].partition_broadcast(P)).then_inc(ln2_in, 16)
                    ac.dma_start(ln2_bt[:, :], ln2_b[0].partition_broadcast(P)).then_inc(ln2_in, 16)
            for t in range(TT):
                ac.wait_ge(sm["ln2_v"], t + 1)
                A.activation(lrs2[:, t, 0:1], lrs2[:, t, 0:1], ACT.Sqrt).then_inc(sm["ln2_s"], 1)
                if t >= 1:
                    ac.wait_ge(sm["ln2_ok"], t)
                    ac.dma_start(out[0, (t - 1) * P:t * P, :], z_tok[:, t - 1, :]).then_inc(sm["out_stored"], 16)
            ac.wait_ge(sm["ln2_ok"], TT)
            ac.dma_start(out[0, (TT - 1) * P:, :], z_tok[:, TT - 1, :]).then_inc(sm["out_stored"], 16)
            ac.wait_ge(sm["out_stored"], 16 * TT)


_INS = ["x", "positions", "w_in", "gla_w_gate_up", "gla_b_gate", "gla_norm_g", "w_gla_o", "mla_q_norm_g", "mla_w_uq",
        "mla_kv_norm_g", "mla_w_ukv", "w_mla_o", "w_out", "ln1_g", "ln1_b", "w_up", "conv_w", "conv_b", "w_down",
        "ln2_g", "ln2_b"]


def kernel(**inputs):
    import numpy as _np
    import concourse.bacc as _bacc
    from concourse import mybir as _mybir
    from concourse.bass_utils import run_bass_kernel_spmd as _run

    nc = _bacc.Bacc("TRN2", target_bir_lowering=False, num_devices=1)
    arrays, args = {}, []
    for name in _INS:
        a = _np.ascontiguousarray(inputs[name])
        arrays[f"in_{name}_dram"] = a
        args.append(nc.dram_tensor(f"in_{name}_dram", a.shape, _mybir.dt.from_np(a.dtype), kind="ExternalInput").ap())
    out = nc.dram_tensor("out_0_dram", (1, S, D), F32, kind="ExternalOutput").ap()
    block_kernel(nc, *args, out)
    r = _run(nc, [arrays], core_ids=[0])
    return r.results[0]["out_0_dram"]
```

```python
from contextlib import ExitStack

import concourse.bass as bass
from concourse import mybir

F32 = mybir.dt.float32
F32R = mybir.dt.float32r
I32 = mybir.dt.int32
ALU = mybir.AluOpType
ACT = mybir.ActivationFunctionType
AX = mybir.AxisListType.X

P = 128
HALF = 512
D, S = 1024, 1024
KT, TT = D // P, S // P
GH, DK, DV, RANK, TAU, CHUNK = 4, 128, 256, 16, 16.0, 64
MH, QR, KR, NOPE, ROPE, MV = 8, 384, 256, 128, 64, 128
QKT, KVT = QR // P, KR // P
DFF = 2816
FT = DFF // P
HR = ROPE // 2
THETA = 10000.0
ALPHA = 2.0 ** 0.25
LN_EPS, RMS_EPS = 1e-5, 1e-6
ATT_SCALE = (NOPE + ROPE) ** -0.5
C_Q = 0
C_K = C_Q + GH * DK
C_V = C_K + GH * DK
C_R = C_V + GH * DV
C_OG = C_R + RANK
C_CQ = C_OG + GH * DV
C_KR = C_CQ + QR + KR
C_GA = C_KR + ROPE
C_GB = C_GA + D
CW = QR + KR + ROPE
LAT = [(0, 240), (240, 240), (480, CW - 480)]
CHUNKS = S // CHUNK
PI = 3.141592653589793


class Chain:

    def __init__(self, eng, sem):
        self.eng, self.sem, self.n = eng, sem, 0

    def done(self, ins):
        ins.then_inc(self.sem, 1)
        self.n += 1
        return self.n

    def wait(self, value=None):
        self.eng.wait_ge(self.sem, self.n if value is None else value)


def block_kernel(nc, x, positions, w_in, gla_w_gate_up, gla_b_gate, gla_norm_g, w_gla_o, mla_q_norm_g,
                 mla_w_uq, mla_kv_norm_g, mla_w_ukv, w_mla_o, w_out, ln1_g, ln1_b, w_up, conv_w, conv_b,
                 w_down, ln2_g, ln2_b, out):
    ctx = ExitStack()
    with ctx:
        def sem(name):
            return ctx.enter_context(nc.semaphore(name))

        def dram(name, shape):
            return nc.dram_tensor(name, shape, F32, kind="Internal").ap()

        psum_all = ctx.enter_context(nc.psum_tensor("psum_all", [P, 8 * HALF], F32))
        psum = [psum_all[:, i * HALF:(i + 1) * HALF] for i in range(8)]

        class Region:

            def __init__(self, start, size):
                self.at, self.end = start, start + size

            def __call__(self, name, shape, dt=F32):
                size = 4
                for s in shape[1:]:
                    size *= s
                t = nc.alloc_sbuf_tensor_at(name, list(shape), dt, offset=self.at)
                self.at += -(-size // 32) * 32
                assert self.at <= self.end, (name, self.at, self.end)
                return t

        KB = 1024
        base = 16512
        RSZ = 92 * KB
        W0 = base
        A0 = W0 + 48 * KB
        R0 = A0 + 64 * KB
        C0 = R0 + RSZ
        wreg = Region(W0, 48 * KB)
        w_raw = [wreg(f"w_raw{i}", [P, 2048]) for i in range(2)]
        w_hi = [wreg(f"w_hi{i}", [P, 2048], F32R) for i in range(2)]
        w_lo = [wreg(f"w_lo{i}", [P, 2048], F32R) for i in range(2)]

        creg = Region(C0, 229344 - C0)
        ident = creg("ident", [P, P])
        mask_att = creg("mask_att", [P, P])
        mask_gla = creg("mask_gla", [P, P])
        zero_col = creg("zero_col", [P, 1])
        b_gate = creg("b_gate", [P, GH])
        norm_g = creg("norm_g", [P, 2])
        lat_g = creg("lat_g", [P, QKT + KVT])
        small = creg("small", [P, 64])
        eps_rms = creg("eps_rms", [P, 1])

        areg = Region(A0, 64 * KB)
        xT_hi = areg("xT_hi", [P, KT, S], F32R)
        xT_lo = areg("xT_lo", [P, KT, S], F32R)
        r = Region(R0, RSZ)
        x_tok = [r(f"x_tok{i}", [P, D]) for i in range(TT)]
        r = Region(R0, RSZ)
        q_raw = r("q_raw", [P, S])
        k_raw = r("k_raw", [P, S])
        gb_b = r("gb_b", [P, S])
        gb_e = r("gb_e", [P, S])
        gb_n = r("gb_n", [P, S])
        q_x = r("q_x", [P, S])
        k_in = r("k_in", [P, S])
        k_up = r("k_up", [P, S])
        og_s = [r(f"og_s{i}", [P, 2, S]) for i in range(2)]
        v_tok = [r(f"v_tok{i}", [P, TT, DV]) for i in range(2)]
        o_tok = r("o_tok", [P, TT, DV])
        rT = r("rT", [RANK, S])
        sig = [r(f"sig{i}", [P, HALF]) for i in range(2)]
        oT_st = [r(f"oT_st{i}", [P, HALF]) for i in range(2)]
        state = r("state", [P, DV])
        att = [r(f"att{i}", [P, P]) for i in range(2)]
        kst = [r(f"kst{i}", [P, P]) for i in range(2)]
        sq_junk = r("sq_junk", [P, DV])
        ss = small[:, 0:8]
        rs = small[:, 8:16]
        b_last = r("b_last", [P, CHUNKS])
        dec = r("dec", [P, CHUNKS])
        dec2 = r("dec2", [P, TT])
        ones64 = r("ones64", [P, CHUNK])
        w_gate = r("w_gate", [RANK, GH * DK])

        d_og = dram("d_og", [GH * DV, S])
        d_sga = dram("d_sga", [D, S])
        d_sgb = dram("d_sgb", [D, S])
        d_m = dram("d_m", [D, S])
        d_qr = dram("d_qr", [MH, P, S])
        d_om = dram("d_om", [MH * MV, S])
        d_h = dram("d_h", [S, D])

        r = Region(R0, RSZ)
        oT_hi = r("oT_hi", [P, KT, S], F32R)
        oT_lo = r("oT_lo", [P, KT, S], F32R)
        ld_st = [r(f"ld_st{i}", [P, S]) for i in range(2)]
        ga_st = [r(f"ga_st{i}", [P, HALF]) for i in range(2)]
        m_st = [r(f"m_st{i}", [P, HALF]) for i in range(2)]
        gsig = [r(f"gsig{i}", [P, HALF]) for i in range(2)]

        a = Region(A0, 64 * KB)
        cT_hi = a("cT_hi", [P, QKT + KVT, S], F32R)
        cT_lo = a("cT_lo", [P, QKT + KVT, S], F32R)
        kA = a("kA", [P, S], F32R)
        kB = a("kB", [P, S], F32R)
        vv = [[a(f"vv{i}{p}", [P, TT, MV], F32R) for p in "hl"] for i in range(2)]
        r = Region(R0, RSZ)
        c_tok = r("c_tok", [P, TT, CW])
        cos = r("cos", [P, TT, HR])
        sin = r("sin", [P, TT, HR])
        kst3 = r("kst3", [P, TT, 3 * ROPE])
        rtmp = r("rtmp", [P, TT, HR])
        rtmp2 = r("rtmp2", [P, TT, HR])
        pos_i = r("pos_i", [P, TT], I32)
        ifreq = r("ifreq", [P, HR])
        junk2 = r("junk2", [P, QR])
        gsig2 = [r(f"gsig2_{i}", [P, HALF]) for i in range(2)]
        r = Region(R0, RSZ)
        qr_rot = [r(f"qr_rot{i}", [P, MH, ROPE]) for i in range(2)]
        qr_tmp = r("qr_tmp", [P, MH, HR])
        qr_tmp2 = r("qr_tmp2", [P, MH, HR])
        qr_hl = [r(f"qr_hl{i}", [P, MH, 2 * ROPE]) for i in range(2)]
        qr_st = [r(f"qr_st{i}", [P, MH, P]) for i in range(2)]
        r = Region(R0, RSZ)
        pT_hi = r("pT_hi", [P, TT, HALF], F32R)
        pT_lo = r("pT_lo", [P, TT, HALF], F32R)
        p_sb = [r(f"p_sb{i}", [P, S]) for i in range(2)]
        p_sb.append(nc.alloc_sbuf_tensor_at("p_sb2", [P, S], F32, offset=R0 + 88 * KB))
        qrA = [r(f"qrA{i}", [P, S], F32R) for i in range(2)]
        om_st = [r(f"om_st{i}", [P, HALF]) for i in range(2)]
        nmax = r("nmax", [P, 2])
        nbias = r("nbias", [P, 2])
        psums = r("psums", [P, 2])
        prec = r("prec", [P, 2])
        r = Region(R0 + 56 * KB, 32 * KB)
        qT, kT = [], []
        for i in range(2):
            qT.append([r(f"qT{i}{p}", [P, S], F32R) for p in "hl"])
            kT.append([r(f"kT{i}{p}", [P, S], F32R) for p in "hl"])

        a = Region(A0, 64 * KB)
        mT = [[a(f"mT{k}{p}", [P, S], F32R) for p in "hl"] for k in range(KT)]
        r = Region(R0, RSZ)
        xm_hi = r("xm_hi", [P, KT, S], F32R)
        xm_lo = r("xm_lo", [P, KT, S], F32R)
        ld2 = [nc.alloc_sbuf_tensor_at(f"ld2_{i}", [P, S], F32, offset=R0 + (56 + 4 * i) * KB) for i in range(2)]
        sgb_st = [r(f"sgb_st{i}", [P, HALF]) for i in range(2)]
        mm_st = [r(f"mm_st{i}", [P, HALF]) for i in range(2)]
        mx = [r(f"mx{i}", [P, HALF]) for i in range(2)]
        a = Region(A0, 64 * KB)
        h_tok = a("h_tok", [P, TT, D])
        ln_g = a("ln1_gain", [P, D])
        ln_b = a("ln1_bias", [P, D])
        bst = a("bst", [P, TT, 12])
        mv = a("mv", [P, TT, 2])
        lrs = a("lrs", [P, TT, 3])
        eps_ln = creg("eps_ln", [P, 1])
        ln_cols = creg("ln_cols", [P, 2, KT])
        cw = creg("cw", [P, 4, 2 * FT])
        f_all = nc.alloc_sbuf_tensor_at("f_all", [P, FT, S], F32, offset=A0)
        r = Region(R0 + 24 * KB, 68 * KB)
        hT_hi = r("hT_hi", [P, KT, S], F32R)
        hT_lo = r("hT_lo", [P, KT, S], F32R)
        up_g = r("up_g", [P, HALF])
        up_v = r("up_v", [P, HALF])
        y_st = [nc.alloc_sbuf_tensor_at(f"y_st{i}", [P, HALF], F32, offset=A0 + (48 + 2 * i) * KB) for i in range(2)]
        cw_rows = nc.alloc_sbuf_tensor_at("cw_rows", [2 * FT, 4, P], F32, offset=R0 + 40 * KB)
        r = Region(R0 + 24 * KB, 68 * KB)
        f_hi = [r(f"f_hi{i}", [P, S], F32R) for i in range(4)]
        f_lo = [r(f"f_lo{i}", [P, S], F32R) for i in range(4)]
        z_tok = r("z_tok", [P, TT, D])
        bst2 = r("bst2", [P, TT, 12])
        mv2 = r("mv2", [P, TT, 2])
        lrs2 = r("lrs2", [P, TT, 3])
        ln2_gt = nc.alloc_sbuf_tensor_at("ln2_gain", [P, D], F32, offset=A0 + 80 * KB)
        ln2_bt = nc.alloc_sbuf_tensor_at("ln2_bias", [P, D], F32, offset=A0 + 84 * KB)

        win = w_in[0].rearrange("(k p) c -> p k c", p=P)

        def raw(n, k, c):
            return w_raw[n % 2][:, 0:k * c].rearrange("p (k c) -> p k c", k=k)

        slots = []

        def slot(name, k, c, *parts):
            slots.append((name, k, c, parts))

        def win_slot(name, c0, c):
            slot(name, KT, c, (0, c, win[:, :, c0:c0 + c]))

        def head_slots(h):
            if h:
                win_slot(("og", h), C_OG + h * DV, DV)
                win_slot(("v", h), C_V + h * DV, DV)
            slot(("qk", h), KT, 2 * DK, (0, DK, win[:, :, C_Q + h * DK:C_Q + (h + 1) * DK]),
                 (DK, DK, win[:, :, C_K + h * DK:C_K + (h + 1) * DK]))

        win_slot(("r", 0), C_R, RANK)
        head_slots(0)
        win_slot(("og", 0), C_OG, DV)
        win_slot(("v", 0), C_V, DV)
        for h in range(GH - 1):
            head_slots(h + 1)
            win_slot(("gb", h), C_GB + h * 256, 256)
        for j in range(4):
            win_slot(("ga", j), C_GA + j * 256, 256)
        for j in range(4):
            slot(("glao", j), KT, 256, (0, 256, w_gla_o[0].rearrange("(k p) c -> p k c", p=P)[:, :, j * 256:(j + 1) * 256]))
        for j, (c0, c) in enumerate(LAT):
            win_slot(("lat", j), C_CQ + c0, c)
        win_slot(("gb", 3), C_GB + 3 * 256, 256)
        uq = mla_w_uq[0].rearrange("(k p) (h c) -> p k h c", p=P, c=NOPE + ROPE)
        ukv = mla_w_ukv[0].rearrange("(k p) (h c) -> p k h c", p=P, c=NOPE + MV)
        slot(("rope", 0), QKT, MH * ROPE, *[(h * ROPE, ROPE, uq[:, :, h, NOPE:]) for h in range(MH)])
        for h in range(MH):
            slots.append((("mla", h), QKT + 2 * KVT, P, (("q", uq[:, :, h, 0:NOPE]), ("k", ukv[:, :, h, 0:NOPE]), ("v", ukv[:, :, h, NOPE:]))))
        for j in range(4):
            slot(("mlao", j), KT, 256, (0, 256, w_mla_o[0].rearrange("(k p) c -> p k c", p=P)[:, :, j * 256:(j + 1) * 256]))
        for j in range(4):
            slot(("wout", j), 4, HALF, (0, HALF, w_out[0].rearrange("(k p) c -> p k c", p=P)[:, j % 2 * 4:j % 2 * 4 + 4, j // 2 * HALF:(j // 2 + 1) * HALF]))
        wup = w_up[0].rearrange("(k p) c -> p k c", p=P)
        for i in range(FT):
            slot(("up", i), KT, 256, (0, P, wup[:, :, i * P:(i + 1) * P]), (P, P, wup[:, :, DFF + i * P:DFF + (i + 1) * P]))
        wdn = w_down[0].rearrange("(k p) c -> p k c", p=P)
        for i in range(FT):
            dh, kk = i // (FT // 2), i % (FT // 2)
            slot(("down", i), 2, HALF, (0, HALF, wdn[:, 2 * kk:2 * kk + 2, dh * HALF:(dh + 1) * HALF]))
        slot_no = {name: n for n, (name, *_) in enumerate(slots)}

        landed_value, total = [], [0, 0]
        for n, (_, k, c, parts) in enumerate(slots):
            total[n % 2] += 16 * len(parts)
            landed_value.append(total[n % 2])

        def w_part(n, k_no, c0, c, lo=False):
            width = slots[n][2]
            t = (w_lo if lo else w_hi)[n % 2]
            return t[:, k_no * width + c0:k_no * width + c0 + c]

        w_landed = [sem("w_landed0"), sem("w_landed1")]
        w_high = sem("w_high")
        w_split = sem("w_split")
        w_used = sem("w_used")
        consts = sem("consts")
        x_landed = [sem(f"x_landed{t}") for t in range(TT)]
        par_landed = sem("par_landed")
        xt_done = sem("xt_done")
        xt_hi = sem("xt_hi")
        xt_lo = sem("xt_lo")
        mm = sem("mm")
        ev_a = sem("ev_a")
        ev_v = sem("ev_v")
        vs = sem("vs")
        as_ = sem("as")

        groups, gid = [], {}

        def group(kind, ev):
            gid[kind] = len(groups)
            groups.append(ev)

        def q4(kind, ev):
            for j in range(4):
                group(kind + (j,), ev)

        for j in range(2):
            group(("r", j), "a")
        q4(("qk", 0), "a")
        q4(("og", 0), "v")
        q4(("v", 0), "a")
        for h in range(GH):
            last = h == GH - 1
            q4(("ga", 0) if last else ("og", h + 1), "a" if last else "v")
            q4(("ga", 1) if last else ("v", h + 1), "a")
            if not last:
                q4(("qk", h + 1), "a")
            q4(("oT", h), "v")
            if not last:
                q4(("gb", h), "a")
        q4(("ga", 2), "a")
        q4(("ga", 3), "a")
        for j in range(4):
            q4(("glao", j), "v")
        for j in range(3):
            for t in range(TT):
                group(("lat", j, t), "a")
        q4(("gb", 3), "a")
        for c in range(QKT + KVT):
            for half in range(2):
                group(("cT", c, half), "v")
        for m in range(2):
            for half in range(2):
                group(("kT", m, half), "a")
        for t in range(TT + 1):
            if t < TT:
                group(("qr", t), "v")
            if t > 0:
                group(("qrT", t - 1, 0), "a")
                group(("qrT", t - 1, 1), "a")
        ev_at, cnt = [], {"a": 0, "v": 0}
        for ev in groups:
            cnt[ev] += 1
            ev_at.append(({"a": ev_a, "v": ev_v}[ev], cnt[ev]))

        def bank(kind):
            return psum[gid[kind] % 4]

        PARAMS = 11

        names = ("gate_mm gate_l gate_scan gate_exp prep_done att_mm att_ok kst_ok ou_mm o_ev st_ev norm_v norm_s "
                 "o_scaled sig_ok lat_sq lat_v lat_s lat_ok hi_ok op_hi op_lo ld_ok rope_q rot_ok kst3_ok sins "
                 "angs s_mm nb_ok p_exp p_norm t_mm pt_hi pt_lo pv_mm om_ev pj_mm pj_hi pj_lo mo_mm mo_ev mix_ok "
                 "ln_n ln_r ln2_n ln2_r ln2_g mix_hi mix_lo wo_mm wo_ev ln_v ln_s ln_ok hT_mm hT_hi hT_lo up_mm up_a up_v up_c up_si up_f fs_hi fs_lo "
                 "dn_mm dn_ev ln2_v ln2_s ln2_ok ad2 vd2 ifr par_mm par_ok og_stored ga_stored m_stored qr_stored "
                 "om_stored h_stored out_stored pos_ok").split()
        sm = {n: sem(n) for n in names}
        sig_st = [sem("sig_st0"), sem("sig_st1")]
        ld_in = [sem("ld_in0"), sem("ld_in1")]
        ga_in = [sem("ga_in0"), sem("ga_in1")]
        m_out = [sem("m_out0"), sem("m_out1")]
        oT_out = [sem("oT_out0"), sem("oT_out1")]
        qs_out = [sem("qs_out0"), sem("qs_out1")]
        qrA_in = [sem("qrA_in0"), sem("qrA_in1")]
        om_out = [sem("om_out0"), sem("om_out1")]
        mx_in = [sem("mx_in0"), sem("mx_in1")]
        row_in = [sem(f"row_in{t}") for t in range(TT)]
        row2_in = [sem(f"row2_in{t}") for t in range(TT)]
        ln1_in, ln2_in = sem("ln1_in"), sem("ln2_in")

        def tgroup(s, g=0):
            h, qb = divmod(s, TT)
            return 12 * h + (qb if qb < 4 else 4 + 2 * (qb - 4)) + g

        STEPS = MH * TT
        FILLED = 6
        EARLY = {57: 0, 58: 1, 59: 2, 60: 3, 61: 4, 62: 6, 64: 5}
        early = list(EARLY.values())
        LASTG = {"r": 1, "og": 3, "v": 3, "qk": 3, "gb": 3, "ga": 3, "glao": 3}

        def used_at(n):
            name, i = slots[n][0]
            if name in LASTG:
                return mm, gid[(name, i, LASTG[name])] + 1 if name != "r" else gid[("r", 1)] + 1
            if name == "lat":
                return mm, gid[("lat", i, TT - 1)] + 1
            if name == "rope":
                return mm, gid[("qr", TT - 1)] + 1
            if name == "mla":
                return sm["pj_mm"], 6 * (i + 1)
            if name == "mlao":
                return sm["mo_mm"], 4 * (i + 1)
            if name == "wout":
                return (sm["wo_mm"], TT * (i // 2 + 1)) if i % 2 else (w_used, i // 2 + 1)
            if name == "up":
                return sm["up_mm"], 4 * (i + 1)
            dh, kk = divmod(i, FT // 2)
            if kk == FT // 2 - 1:
                return sm["dn_mm"], TT * (dh + 1)
            return w_used, 2 + dh * (FT // 2 - 1) + kk + 1

        block = ctx.enter_context(nc.Block())

        @block.sync
        def _(sp):
            for t in range(TT):
                sp.dma_start(x_tok[t][:, :], x[0, t * P:(t + 1) * P, :]).then_inc(x_landed[t], 16)
            for n, (name, k, c, parts) in enumerate(slots):
                if n >= 2:
                    sp.wait_ge(w_split, n - 1)
                if name[0] == "mla":
                    at = 0
                    for what, src in parts:
                        kk = QKT if what == "q" else KVT
                        dst = w_raw[n % 2][:, at * P:(at + kk) * P].rearrange("p (k c) -> p k c", k=kk)
                        sp.dma_start(dst, src).then_inc(w_landed[n % 2], 16)
                        at += kk
                    continue
                for c0, cc, src in parts:
                    sp.dma_start(raw(n, k, c)[:, :, c0:c0 + cc], src).then_inc(w_landed[n % 2], 16)

        @block.gpsimd
        def _(pool):
            ms = Chain(pool, consts)
            ms.done(nc.gpsimd.memset(zero_col[:, :], 0.0))
            ms.done(nc.gpsimd.memset(ident[:, :], 1.0))
            ms.done(nc.gpsimd.memset(mask_att[:, :], 0.0))
            ms.done(nc.gpsimd.memset(mask_gla[:, :], 1.0))
            ms.wait()
            ms.done(nc.gpsimd.affine_select(ident[:, :], ident[:, :], pattern=[[-1, P]], compare_op=ALU.is_equal,
                                            fill=0.0, base=0, channel_multiplier=1))
            ms.done(nc.gpsimd.affine_select(mask_att[:, :], mask_att[:, :], pattern=[[-1, P]], compare_op=ALU.is_ge,
                                            fill=-1e30, base=0, channel_multiplier=1))
            ms.done(nc.gpsimd.affine_select(mask_gla[:, :], mask_gla[:, :], pattern=[[1, P]], compare_op=ALU.is_ge,
                                            fill=0.0, base=0, channel_multiplier=-1))
            ms.wait()
            ms.done(nc.gpsimd.memset(mask_gla[0:CHUNK, CHUNK:P], 0.0))
            ms.done(nc.gpsimd.memset(ones64[:, :], 1.0))
            ms.done(nc.gpsimd.memset(eps_rms[:, :], RMS_EPS))
            ms.done(nc.gpsimd.memset(eps_ln[:, :], LN_EPS))
            for n, (name, k, c, parts) in enumerate(slots):
                w = k * c
                pool.wait_ge(w_landed[n % 2], landed_value[n])
                if n >= 2:
                    pool.wait_ge(*used_at(n - 2))
                nc.gpsimd.tensor_copy(w_hi[n % 2][:, 0:w], w_raw[n % 2][:, 0:w]).then_inc(w_high, 1)
                pool.wait_ge(w_high, n + 1)
                nc.gpsimd.tensor_tensor(w_lo[n % 2][:, 0:w], w_raw[n % 2][:, 0:w],
                                        w_hi[n % 2][:, 0:w].bitcast(F32), ALU.subtract).then_inc(w_split, 1)
            for t in range(TT):
                pool.wait_ge(sm["ln2_g"], t + 1)
                nc.gpsimd.tensor_tensor(z_tok[:, t, :], z_tok[:, t, :], ln2_bt[:, :], ALU.add).then_inc(sm["ln2_ok"], 1)

        @block.tensor
        def _(pe):
            def free(kind):
                g = gid[kind]
                if g >= 4:
                    pe.wait_ge(*ev_at[g - 4])

            def split3(out_ap, terms, start=True, stop=True):
                for i, (ah, al, bh, bl) in enumerate(terms):
                    pe.matmul(out_ap, ah, bh, start=start and i == 0, stop=False)
                    pe.matmul(out_ap, ah, bl, start=False, stop=False)
                    last = pe.matmul(out_ap, al, bh, start=False, stop=stop and i == len(terms) - 1)
                return last

            def need(name):
                n = slot_no[name]
                pe.wait_ge(w_split, n + 1)
                return n

            def feature_group(kind, n, tile, half, th, tl, kts=KT):
                free(kind)
                last = split3(bank(kind), [(w_part(n, k, tile * P, P), w_part(n, k, tile * P, P, True),
                                            th[:, k, half * HALF:(half + 1) * HALF], tl[:, k, half * HALF:(half + 1) * HALF])
                                           for k in range(kts)])
                last.then_inc(mm, 1)
                return last

            def features(kind, name, th, tl, js=range(4)):
                n = need(name)
                for j in js:
                    feature_group(kind + (j,), n, j // 2, j % 2, th, tl)

            def v_groups(h, js=range(4)):
                n = need(("v", h))
                for j in js:
                    kind = ("v", h, j)
                    free(kind)
                    for i in range(2):
                        t = 2 * j + i
                        last = split3(bank(kind)[:, i * DV:(i + 1) * DV],
                                      [(xT_hi[:, k, t * P:(t + 1) * P], xT_lo[:, k, t * P:(t + 1) * P],
                                        w_part(n, k, 0, DV), w_part(n, k, 0, DV, True)) for k in range(KT)])
                    last.then_inc(mm, 1)

            def transposes(kind, srcs):
                free(kind)
                for i, s_ap in enumerate(srcs):
                    last = pe.transpose(bank(kind)[:, i * P:(i + 1) * P], s_ap, ident[:, :])
                last.then_inc(mm, 1)

            def gates(h):
                if h == 0:
                    pe.wait_ge(par_landed, 16 * PARAMS)
                    pe.wait_ge(*ev_at[gid[("r", 1)]])
                else:
                    pe.wait_ge(sm["att_ok"], TT * h)
                    pe.wait_ge(sm["kst_ok"], TT * h)
                    pe.wait_ge(sm["o_ev"], TT * h)
                for half in range(2):
                    last = pe.matmul(psum[4 + half], w_gate[:, h * DK:(h + 1) * DK], rT[:, half * HALF:(half + 1) * HALF],
                                     start=True, stop=True)
                last.then_inc(sm["gate_mm"], 1)

            def att_part(h, t):
                i = h * TT + t
                c = slice(t * P, (t + 1) * P)
                if i >= 1:
                    pe.wait_ge(sm["att_ok"], i)
                    pe.wait_ge(sm["kst_ok"], i)
                pe.matmul(psum[4][:, 0:P], k_in[:, c], q_raw[:, c], start=True, stop=True)
                pe.matmul(psum[4][0:CHUNK, P:P + CHUNK], k_raw[:, t * P:t * P + CHUNK], q_raw[:, t * P + CHUNK:(t + 1) * P],
                          start=True, stop=True)
                pe.transpose(psum[7][:, 0:P], k_up[:, c], ident[:, :]).then_inc(sm["att_mm"], 1)

            def out_part(h, t):
                i = h * TT + t
                pe.wait_ge(sm["att_ok"], i + 1)
                if i >= 1:
                    pe.wait_ge(sm["o_ev"], i)
                    pe.wait_ge(sm["st_ev"], i)
                pe.matmul(psum[5][:, 0:DV], att[i % 2][:, :], v_tok[h % 2][:, t, :], start=True, stop=t == 0)
                if t > 0:
                    pe.matmul(psum[5][:, 0:DV], q_x[:, t * P:(t + 1) * P], state[:, :], start=False, stop=True)
                pe.wait_ge(sm["kst_ok"], i + 1)
                pe.matmul(psum[6][:, 0:DV], kst[i % 2][:, :], v_tok[h % 2][:, t, :], start=True, stop=True).then_inc(sm["ou_mm"], 1)

            pe.wait_ge(consts, 7)
            for t in range(TT):
                pe.wait_ge(x_landed[t], 16)
                for g in range(2):
                    i = 2 * t + g
                    if i >= 4:
                        pe.wait_ge(xt_lo, i - 3)
                    for j in range(4):
                        last = pe.transpose(psum[i % 4][:, j * P:(j + 1) * P], x_tok[t][:, (4 * g + j) * P:(4 * g + j + 1) * P], ident[:, :])
                    last.then_inc(xt_done, 1)
            pe.wait_ge(par_landed, 16 * PARAMS)
            for k in range(4):
                last = pe.transpose(psum[7][:, k * 2 * FT:(k + 1) * 2 * FT], cw_rows[:, k, :], ident[0:2 * FT, 0:2 * FT])
            last.then_inc(sm["par_mm"], 1)
            pe.wait_ge(xt_lo, 2 * TT)
            n = need(("r", 0))
            for half in range(2):
                kind = ("r", half)
                last = split3(bank(kind)[0:RANK, :], [(w_part(n, k, 0, RANK), w_part(n, k, 0, RANK, True),
                                                       xT_hi[:, k, half * HALF:(half + 1) * HALF], xT_lo[:, k, half * HALF:(half + 1) * HALF])
                                                      for k in range(KT)])
                last.then_inc(mm, 1)
            features(("qk", 0), ("qk", 0), xT_hi, xT_lo)
            gates(0)
            features(("og", 0), ("og", 0), xT_hi, xT_lo)
            v_groups(0)
            for h in range(GH):
                last_head = h == GH - 1
                pe.wait_ge(sm["prep_done"], h + 1)
                pe.wait_ge(*ev_at[gid[("v", h, 3)]])
                for t in range(TT):
                    att_part(h, t)
                    if last_head:
                        features(("ga", t // 4), ("ga", t // 4), xT_hi, xT_lo, [t % 4])
                    elif t < 4:
                        features(("og", h + 1), ("og", h + 1), xT_hi, xT_lo, [t])
                    else:
                        v_groups(h + 1, [t - 4])
                    out_part(h, t)
                if not last_head:
                    gates(h + 1)
                    features(("qk", h + 1), ("qk", h + 1), xT_hi, xT_lo)
                pe.wait_ge(sm["o_scaled"], h + 1)
                for j in range(4):
                    vt, half = divmod(j, 2)
                    transposes(("oT", h, j), [o_tok[:, 4 * half + i, vt * P:(vt + 1) * P] for i in range(4)])
                if not last_head:
                    features(("gb", h), ("gb", h), xT_hi, xT_lo)
            features(("ga", 2), ("ga", 2), xT_hi, xT_lo)
            features(("ga", 3), ("ga", 3), xT_hi, xT_lo)
            pe.wait_ge(sm["op_lo"], KT)
            for j in range(4):
                features(("glao", j), ("glao", j), oT_hi, oT_lo)
            for j, (c0, c) in enumerate(LAT):
                n = need(("lat", j))
                for t in range(TT):
                    kind = ("lat", j, t)
                    free(kind)
                    split3(bank(kind)[:, 0:c], [(xT_hi[:, k, t * P:(t + 1) * P], xT_lo[:, k, t * P:(t + 1) * P],
                                                 w_part(n, k, 0, c), w_part(n, k, 0, c, True)) for k in range(KT)]).then_inc(mm, 1)
            features(("gb", 3), ("gb", 3), xT_hi, xT_lo)
            pe.wait_ge(sm["lat_ok"], 1)
            for c in range(QKT + KVT):
                for half in range(2):
                    transposes(("cT", c, half), [c_tok[:, 4 * half + i, c * P:(c + 1) * P] for i in range(4)])
            pe.wait_ge(sm["kst3_ok"], 1)
            for m in range(2):
                for half in range(2):
                    c0 = ROPE if m == 0 else 0
                    transposes(("kT", m, half), [kst3[:, 4 * half + i, c0:c0 + P] for i in range(4)])
            def project(h, j):
                n = need(("mla", h))
                pe.wait_ge(sm["pj_lo"], 6 * h + j) if 6 * h + j else None
                if j < 4:
                    half, kts, k0, c0 = j % 2, (QKT, KVT)[j // 2], (0, QKT)[j // 2], (0, QKT)[j // 2]
                    last = split3(psum[7], [(w_part(n, c0 + k, 0, P), w_part(n, c0 + k, 0, P, True),
                                             cT_hi[:, k0 + k, half * HALF:(half + 1) * HALF], cT_lo[:, k0 + k, half * HALF:(half + 1) * HALF])
                                            for k in range(kts)])
                else:
                    for i in range(4):
                        t = 4 * (j - 4) + i
                        last = split3(psum[7][:, i * P:(i + 1) * P],
                                      [(cT_hi[:, QKT + k, t * P:(t + 1) * P], cT_lo[:, QKT + k, t * P:(t + 1) * P],
                                        w_part(n, QKT + KVT + k, 0, P), w_part(n, QKT + KVT + k, 0, P, True)) for k in range(KVT)])
                last.then_inc(sm["pj_mm"], 1)
    
            n = need(("rope", 0))
            pe.wait_ge(*ev_at[gid[("cT", QKT + KVT - 1, 1)]])
            for t in range(TT + 1):
                if t < TT:
                    kind = ("qr", t)
                    free(kind)
                    split3(bank(kind), [(cT_hi[:, k, t * P:(t + 1) * P], cT_lo[:, k, t * P:(t + 1) * P],
                                         w_part(n, k, 0, HALF), w_part(n, k, 0, HALF, True)) for k in range(QKT)]).then_inc(mm, 1)
                if t < 6:
                    project(0, t)
                if t > 0:
                    pe.wait_ge(sm["rot_ok"], t)
                    for g in range(2):
                        transposes(("qrT", t - 1, g), [qr_hl[(t - 1) % 2][:, 4 * g + i, :] for i in range(4)])

            def scores(s):
                h, qb = divmod(s, TT)
                q = slice(qb * P, (qb + 1) * P)
                if qb == 0:
                    pe.wait_ge(sm["pj_lo"], 6 * (h + 1))
                    pe.wait_ge(qrA_in[h % 2], 16 * (h // 2 + 1))
                if s >= 2:
                    pe.wait_ge(sm["p_exp"], s - 1)
                w = (qb + 1) * P
                qh, ql = qT[h % 2]
                kh, kl = kT[h % 2]
                for c0 in range(0, w, HALF):
                    c = slice(c0, min(w, c0 + HALF))
                    o = psum_all[:, (s % 2) * S + c.start:(s % 2) * S + c.stop]
                    pe.matmul(o, qh[:, q], kh[:, c], start=True, stop=False)
                    pe.matmul(o, qh[:, q], kl[:, c], start=False, stop=False)
                    pe.matmul(o, ql[:, q], kh[:, c], start=False, stop=False)
                    pe.matmul(o, qrA[h % 2][:, q], kA[:, c], start=False, stop=False)
                    last = pe.matmul(o, qrA[h % 2][:, q], kB[:, c], start=False, stop=True)
                last.then_inc(sm["s_mm"], 1)

            def probs_t(s):
                h, qb = divmod(s, TT)
                pe.wait_ge(sm["p_norm"], s + 1)
                for g in range(1 if qb < 4 else 2):
                    tg = tgroup(s, g)
                    if tg >= 2:
                        pe.wait_ge(sm["pt_lo"], tg - 1)
                    for kb in range(4 * g, min(qb + 1, 4 * g + 4)):
                        last = pe.transpose(psum[4 + tg % 2][:, (kb - 4 * g) * P:(kb - 4 * g + 1) * P],
                                            p_sb[s % 3][:, kb * P:(kb + 1) * P], ident[:, :])
                    last.then_inc(sm["t_mm"], 1)

            def values(s):
                h, qb = divmod(s, TT)
                sb = qb // 4
                pe.wait_ge(sm["pt_lo"], tgroup(s, 0 if qb < 4 else 1) + 1)
                n = 2 * h + sb
                if n >= 1:
                    pe.wait_ge(sm["om_ev"], n)
                vh, vl = vv[h % 2]
                for kb in range(4 * sb + 4):
                    c = slice(max(0, kb - 4 * sb) * P, HALF)
                    pe.matmul(psum[6][:, c], vh[:, kb, :], pT_hi[:, kb, c], start=kb == 0, stop=False)
                    pe.matmul(psum[6][:, c], vh[:, kb, :], pT_lo[:, kb, c], start=False, stop=False)
                    last = pe.matmul(psum[6][:, c], vl[:, kb, :], pT_hi[:, kb, c], start=False, stop=kb == 4 * sb + 3)
                last.then_inc(sm["pv_mm"], 1)

            pe.wait_ge(*ev_at[-1])
            pe.wait_ge(*ev_at[-3])
            for s in range(STEPS + 3):
                h, qb = divmod(s, TT)
                if s < STEPS:
                    scores(s)
                if h + 1 < MH and qb < FILLED:
                    project(h + 1, qb)
                if s >= 3 and (s - 3) % 4 == 3:
                    values(s - 3)
                if 2 <= s < STEPS + 2:
                    probs_t(s - 2)

            pe.wait_ge(sm["ad2"], KT + 1)
            for j in range(4):
                n = need(("mlao", j))
                for jj in range(4):
                    g = 4 * j + jj
                    if g >= 4:
                        pe.wait_ge(sm["mo_ev"], g - 3)
                    split3(psum[g % 4], [(w_part(n, k, jj // 2 * P, P), w_part(n, k, jj // 2 * P, P, True),
                                          mT[k][0][:, jj % 2 * HALF:(jj % 2 + 1) * HALF], mT[k][1][:, jj % 2 * HALF:(jj % 2 + 1) * HALF])
                                         for k in range(KT)]).then_inc(sm["mo_mm"], 1)
            pe.wait_ge(sm["mix_lo"], 16)
            for dh in range(2):
                for part in range(2):
                    n = need(("wout", 2 * dh + part))
                    for t in range(TT):
                        if dh == 1 and part == 0:
                            pe.wait_ge(sm["wo_ev"], t + 1)
                        last = split3(psum[t], [(xm_hi[:, 4 * part + k, t * P:(t + 1) * P], xm_lo[:, 4 * part + k, t * P:(t + 1) * P],
                                                 w_part(n, k, 0, HALF), w_part(n, k, 0, HALF, True)) for k in range(4)],
                                      start=part == 0, stop=part == 1)
                        if part == 1:
                            last.then_inc(sm["wo_mm"], 1)
                        elif t == TT - 1:
                            last.then_inc(w_used, 1)
            def rows_t(half, ks):
                for k in ks:
                    i = KT * half + k
                    if i >= 4:
                        pe.wait_ge(sm["hT_lo"], i - 3)
                    for j in range(4):
                        last = pe.transpose(psum[4 + i % 4][:, j * P:(j + 1) * P], h_tok[:, 4 * half + j, k * P:(k + 1) * P], ident[:, :])
                    last.then_inc(sm["hT_mm"], 1)

            def up_group(i, half, part):
                n = need(("up", i))
                split3(psum[4 * (i % 2) + 2 * part + half],
                       [(w_part(n, k, part * P, P), w_part(n, k, part * P, P, True),
                         hT_hi[:, k, half * HALF:(half + 1) * HALF], hT_lo[:, k, half * HALF:(half + 1) * HALF])
                        for k in range(KT)]).then_inc(sm["up_mm"], 1)

            pe.wait_ge(sm["wo_ev"], 2 * TT)
            pe.wait_ge(sm["ln_n"], 4)
            rows_t(0, range(KT))
            pe.wait_ge(sm["hT_lo"], KT)
            up_group(0, 0, 0)
            pe.wait_ge(sm["ln_n"], TT)
            rows_t(1, range(4))
            up_group(0, 0, 1)
            rows_t(1, range(4, KT))
            pe.wait_ge(sm["hT_lo"], 2 * KT)
            up_group(0, 1, 0)
            up_group(0, 1, 1)
            for i in range(1, FT):
                if i >= 2:
                    pe.wait_ge(sm["up_c"], 4 * (i - 1))
                for half in range(2):
                    for part in range(2):
                        up_group(i, half, part)
            def down(i, t):
                dh, kk = divmod(i, FT // 2)
                n = need(("down", i))
                pe.wait_ge(sm["fs_lo"], 2 * i + 2)
                u = 2 * i
                last = split3(psum[t], [(f_hi[(u + k) % 4][:, t * P:(t + 1) * P], f_lo[(u + k) % 4][:, t * P:(t + 1) * P],
                                         w_part(n, k, 0, HALF), w_part(n, k, 0, HALF, True)) for k in range(2)],
                              start=kk == 0, stop=kk == FT // 2 - 1)
                if kk == FT // 2 - 1:
                    last.then_inc(sm["dn_mm"], 1)
                elif t == TT - 1:
                    last.then_inc(w_used, 1)

            for i in range(FT - 2):
                for t in range(TT):
                    if i == 0:
                        pe.wait_ge(sm["up_c"], 4 * FT)
                    if i == FT // 2:
                        pe.wait_ge(sm["dn_ev"], t + 1)
                    down(i, t)
            for t in range(TT):
                down(FT - 2, t)
                down(FT - 1, t)

        @block.vector
        def _(ve):
            vc = Chain(ve, vs)

            def op(ins):
                vc.done(ins)
                vc.wait()

            def split_lo(lo, src, hi, s_=None):
                return nc.vector.tensor_tensor(lo, src, hi.bitcast(F32), ALU.subtract)

            V = nc.vector
            ve.wait_ge(consts, 11)
            for t in range(TT):
                for g in range(2):
                    i = 2 * t + g
                    ve.wait_ge(xt_hi, i + 1)
                    c = slice(t * P, (t + 1) * P)
                    split_lo(xT_lo[:, 4 * g:4 * g + 4, c], psum[i % 4].rearrange("p (a b) -> p a b", a=4),
                             xT_hi[:, 4 * g:4 * g + 4, c]).then_inc(xt_lo, 1)
            ve.wait_ge(sm["par_mm"], 1)
            V.tensor_copy(cw[:, :, :], psum[7][:, 0:8 * FT].rearrange("p (a b) -> p a b", a=4)).then_inc(sm["par_ok"], 1)

            n_sig = [0]

            def og_group(h, j):
                vt, half = divmod(j, 2)
                n_sig[0] += 1
                ve.wait_ge(sm["sig_ok"], n_sig[0])
                V.scalar_tensor_tensor(og_s[h % 2][:, vt, half * HALF:(half + 1) * HALF], bank(("og", h, j)), norm_g[:, vt:vt + 1],
                                       sig[(n_sig[0] - 1) % 2][:, :], ALU.mult, ALU.mult).then_inc(ev_v, 1)

            def gate_sums(h):
                ve.wait_ge(sm["gate_l"], h + 1)
                op(V.scalar_tensor_tensor(gb_n[:, :], gb_b[:, :], 0.0, gb_e[:, :], ALU.min, ALU.subtract))
                for c in range(CHUNKS):
                    cc = slice(c * CHUNK, (c + 1) * CHUNK)
                    vc.done(V.tensor_tensor_scan(gb_b[:, cc], ones64[:, :], gb_n[:, cc], 0.0, ALU.mult, ALU.add))
                vc.wait()
                b3 = gb_b[:, :].rearrange("p (c i) -> p c i", i=CHUNK)
                n3 = gb_n[:, :].rearrange("p (c i) -> p c i", i=CHUNK)
                op(V.tensor_copy(b_last[:, :], b3[:, :, CHUNK - 1]))
                V.tensor_tensor(n3, b_last[:, :].unsqueeze(2).broadcast_to((P, CHUNKS, CHUNK)), b3, ALU.subtract).then_inc(sm["gate_scan"], 1)

            def prep(h):
                ve.wait_ge(sm["gate_exp"], h + 1)
                ve.wait_ge(*ev_at[gid[("qk", h, 3)]])
                op(V.scalar_tensor_tensor(q_raw[:, :], q_raw[:, :], DK ** -0.5, gb_e[:, :], ALU.mult, ALU.mult))
                vc.done(V.tensor_tensor(k_in[:, :], k_raw[:, :], gb_b[:, :], ALU.mult))
                vc.wait()
                op(V.tensor_tensor(k_raw[:, :], k_raw[:, :], gb_n[:, :], ALU.mult))
                q4v = q_raw[:, :].rearrange("p (t c i) -> p t c i", c=2, i=CHUNK)
                x4v = q_x[:, :].rearrange("p (t c i) -> p t c i", c=2, i=CHUNK)
                k4v = k_raw[:, :].rearrange("p (t c i) -> p t c i", c=2, i=CHUNK)
                u4v = k_up[:, :].rearrange("p (t c i) -> p t c i", c=2, i=CHUNK)
                d2 = dec[:, :].rearrange("p (t c) -> p t c", c=2)
                vc.done(V.tensor_copy(x4v[:, :, 0, :], q4v[:, :, 0, :]))
                vc.done(V.tensor_tensor(x4v[:, :, 1, :], q4v[:, :, 1, :], d2[:, :, 0].unsqueeze(2).broadcast_to((P, TT, CHUNK)), ALU.mult))
                vc.done(V.tensor_copy(u4v[:, :, 1, :], k4v[:, :, 1, :]))
                vc.done(V.tensor_tensor(u4v[:, :, 0, :], k4v[:, :, 0, :], d2[:, :, 1].unsqueeze(2).broadcast_to((P, TT, CHUNK)), ALU.mult))
                V.tensor_tensor(dec2[:, :], d2[:, :, 0], d2[:, :, 1], ALU.mult).then_inc(sm["prep_done"], 1)

            def att_mask(h, t):
                i = h * TT + t
                ve.wait_ge(sm["att_mm"], i + 1)
                if i >= 2:
                    ve.wait_ge(sm["ou_mm"], i - 1)
                a = att[i % 2]
                op(V.tensor_scalar(a[:, :], psum[4][:, 0:P], 3.0e38, -3.0e38, ALU.min, ALU.max))
                op(V.tensor_tensor(a[:, :], a[:, :], mask_gla[:, :], ALU.mult))
                V.tensor_copy(a[0:CHUNK, CHUNK:P], psum[4][0:CHUNK, P:P + CHUNK]).then_inc(sm["att_ok"], 1)

            def state_up(h, t):
                i = h * TT + t
                ve.wait_ge(sm["ou_mm"], i + 1)
                if t == 0:
                    V.tensor_copy(state[:, :], psum[6][:, 0:DV]).then_inc(sm["st_ev"], 1)
                else:
                    ve.wait_ge(sm["st_ev"], i)
                    V.scalar_tensor_tensor(state[:, :], state[:, :], dec2[:, t:t + 1], psum[6][:, 0:DV], ALU.mult, ALU.add).then_inc(sm["st_ev"], 1)

            gate_sums(0)
            prep(0)
            for j in range(4):
                og_group(0, j)
            for h in range(GH):
                for t in range(TT):
                    att_mask(h, t)
                    if h < GH - 1 and t < 4:
                        og_group(h + 1, t)
                    state_up(h, t)
                ve.wait_ge(sm["o_ev"], TT * (h + 1))
                V.tensor_scalar(rs, ss, 1.0 / DV, RMS_EPS, ALU.mult, ALU.add).then_inc(sm["norm_v"], 1)
                ve.wait_ge(sm["norm_s"], h + 1)
                op(V.reciprocal(rs, rs))
                V.tensor_tensor(o_tok[:, :, :], o_tok[:, :, :], rs.unsqueeze(2).broadcast_to((P, TT, DV)), ALU.mult).then_inc(sm["o_scaled"], 1)
                if h < GH - 1:
                    gate_sums(h + 1)
                for j in range(4):
                    vt, half = divmod(j, 2)
                    u = 4 * h + j
                    kind = ("oT", h, j)
                    ve.wait_ge(mm, gid[kind] + 1)
                    if u >= 2:
                        ve.wait_ge(oT_out[u % 2], 16 * (u // 2))
                    V.tensor_tensor(oT_st[u % 2][:, :], bank(kind), og_s[h % 2][:, vt, half * HALF:(half + 1) * HALF], ALU.mult).then_inc(ev_v, 1)
                if h < GH - 1:
                    prep(h + 1)

            for k in range(KT):
                ve.wait_ge(sm["op_hi"], k + 1)
                split_lo(oT_lo[:, k, :], ld_st[k % 2][:, :], oT_hi[:, k, :]).then_inc(sm["op_lo"], 1)
            for g in range(16):
                j, jj = divmod(g, 4)
                kind = ("glao", j, jj)
                ve.wait_ge(mm, gid[kind] + 1)
                ve.wait_ge(ga_in[g % 2], 16 * (g // 2 + 1))
                if g >= 2:
                    ve.wait_ge(m_out[g % 2], 16 * (g // 2))
                V.tensor_tensor(m_st[g % 2][:, :], bank(kind), ga_st[g % 2][:, :], ALU.mult).then_inc(ev_v, 1)

            MAGIC = 12582912.0
            C1 = 6.28125
            C2 = 0.0019350051879882812
            C3 = 2 * PI - C1 - C2
            ve.wait_ge(m_out[0], 16 * 8)
            ve.wait_ge(m_out[1], 16 * 8)
            for i in range(HR):
                vc.done(V.memset(ifreq[:, i:i + 1], THETA ** (-i / HR)))
            ve.wait_ge(sm["pos_ok"], 16)
            op(V.tensor_copy(rs, pos_i[:, :]))
            f3 = (P, TT, HR)
            op(V.tensor_tensor(rtmp[:, :, :], rs.unsqueeze(2).broadcast_to(f3), ifreq[:, :].unsqueeze(1).broadcast_to(f3), ALU.mult))
            for tab, quarter in ((sin, 0.0), (cos, 0.25)):
                op(V.tensor_scalar(rtmp2[:, :, :], rtmp[:, :, :], 1.0 / (2 * PI), quarter, ALU.mult, ALU.add))
                op(V.tensor_scalar(rtmp2[:, :, :], rtmp2[:, :, :], MAGIC, None, ALU.add))
                op(V.tensor_scalar(rtmp2[:, :, :], rtmp2[:, :, :], MAGIC, None, ALU.subtract))
                op(V.scalar_tensor_tensor(tab[:, :, :], rtmp2[:, :, :], -C1, rtmp[:, :, :], ALU.mult, ALU.add))
                op(V.scalar_tensor_tensor(tab[:, :, :], rtmp2[:, :, :], -C2, tab[:, :, :], ALU.mult, ALU.add))
                op(V.scalar_tensor_tensor(tab[:, :, :], rtmp2[:, :, :], -C3, tab[:, :, :], ALU.mult, ALU.add))
                if quarter:
                    op(V.tensor_scalar(tab[:, :, :], tab[:, :, :], PI / 2, None, ALU.add))
                V.tensor_scalar(tab[:, :, :], tab[:, :, :], 3.1415925, -3.1415925, ALU.min, ALU.max).then_inc(sm["angs"], 1)

            ve.wait_ge(sm["lat_sq"], 2 * TT)
            rq, rk = small[:, 16:24], small[:, 24:32]
            vc.done(V.tensor_scalar(rq, rq, 1.0 / QR, RMS_EPS, ALU.mult, ALU.add))
            V.tensor_scalar(rk, rk, 1.0 / KR, RMS_EPS, ALU.mult, ALU.add).then_inc(sm["lat_v"], 1)
            ve.wait_ge(sm["lat_s"], 1)
            op(V.reciprocal(small[:, 16:32], small[:, 16:32]))
            vc.done(V.tensor_tensor(c_tok[:, :, 0:QR], c_tok[:, :, 0:QR], rq.unsqueeze(2).broadcast_to((P, TT, QR)), ALU.mult))
            V.tensor_tensor(c_tok[:, :, QR:QR + KR], c_tok[:, :, QR:QR + KR], rk.unsqueeze(2).broadcast_to((P, TT, KR)), ALU.mult).then_inc(sm["lat_ok"], 1)

            def rotate(x1, x2, cs, sn, r1, r2, t1, t2, last_read):
                vc.done(V.tensor_tensor(t1, x1, cs, ALU.mult))
                vc.done(V.tensor_tensor(t2, x2, sn, ALU.mult))
                vc.wait()
                op(V.tensor_tensor(r1, t1, t2, ALU.subtract))
                vc.done(V.tensor_tensor(t1, x2, cs, ALU.mult))
                last_read(V.tensor_tensor(t2, x1, sn, ALU.mult))
                op(V.tensor_tensor(r2, t1, t2, ALU.add))

            ve.wait_ge(sm["sins"], 2)
            kr0 = QR + KR
            rot = c_tok[:, :, kr0:kr0 + ROPE]

            def chain_read(ins):
                vc.done(ins)
                vc.wait()

            rotate(c_tok[:, :, kr0:kr0 + HR], c_tok[:, :, kr0 + HR:kr0 + ROPE], cos[:, :, :], sin[:, :, :],
                   kst3[:, :, 0:HR], kst3[:, :, HR:ROPE], rtmp[:, :, :], rtmp2[:, :, :], chain_read)
            op(V.tensor_copy(rot, kst3[:, :, 0:ROPE]))
            op(V.tensor_copy(kst3[:, :, 0:ROPE].bitcast(F32R), rot))
            vc.done(V.tensor_tensor(kst3[:, :, ROPE:2 * ROPE].bitcast(F32R), rot, kst3[:, :, 0:ROPE], ALU.subtract))
            V.tensor_copy(kst3[:, :, 2 * ROPE:3 * ROPE], kst3[:, :, 0:ROPE]).then_inc(sm["kst3_ok"], 1)
            for c in range(QKT + KVT):
                for half in range(2):
                    hs = slice(half * HALF, (half + 1) * HALF)
                    ve.wait_ge(sm["hi_ok"], 2 * c + half + 1)
                    V.scalar_tensor_tensor(cT_lo[:, c, hs], bank(("cT", c, half)), lat_g[:, c:c + 1], cT_hi[:, c, hs].bitcast(F32),
                                           ALU.mult, ALU.subtract).then_inc(ev_v, 1)
            def pj_low(h, j):
                ve.wait_ge(sm["pj_hi"], 6 * h + j + 1)
                kind, half = divmod(j, 2)
                dst = (qT, kT, vv)[kind][h % 2]
                if kind < 2:
                    hs = slice(half * HALF, (half + 1) * HALF)
                    split_lo(dst[1][:, hs], psum[7], dst[0][:, hs]).then_inc(sm["pj_lo"], 1)
                else:
                    ts = slice(4 * half, 4 * half + 4)
                    split_lo(dst[1][:, ts, :], psum[7].rearrange("p (a b) -> p a b", a=4), dst[0][:, ts, :]).then_inc(sm["pj_lo"], 1)

            h3 = (P, MH, HR)
            for t in range(TT):
                ve.wait_ge(mm, gid[("qr", t)] + 1)
                if t >= 2:
                    ve.wait_ge(mm, gid[("qrT", t - 2, 1)] + 1)
                b3 = bank(("qr", t)).rearrange("p (h c) -> p h c", h=MH)
                R_ = qr_rot[t % 2]

                def bank_read(ins):
                    ins.then_inc(ev_v, 1)
                    ve.wait_ge(*ev_at[gid[("qr", t)]])

                rotate(b3[:, :, 0:HR], b3[:, :, HR:ROPE], cos[:, t, :].unsqueeze(1).broadcast_to(h3), sin[:, t, :].unsqueeze(1).broadcast_to(h3),
                       R_[:, :, 0:HR], R_[:, :, HR:ROPE], qr_tmp[:, :, :], qr_tmp2[:, :, :], bank_read)
                op(V.tensor_copy(qr_hl[t % 2][:, :, 0:ROPE].bitcast(F32R), R_[:, :, :]))
                V.tensor_tensor(qr_hl[t % 2][:, :, ROPE:2 * ROPE].bitcast(F32R), R_[:, :, :], qr_hl[t % 2][:, :, 0:ROPE], ALU.subtract).then_inc(sm["rot_ok"], 1)
                if t < 6:
                    pj_low(0, t)

            for s in range(STEPS + 2):
                h, qb = divmod(s, TT)
                w = (qb + 1) * P
                b0 = (s % 2) * S
                if s < STEPS:
                    ve.wait_ge(sm["s_mm"], s + 1)
                    d = psum_all[:, b0 + w - P:b0 + w]
                    op(V.tensor_tensor(d, d, mask_att[:, :], ALU.add))
                    op(V.tensor_reduce(nmax[:, s % 2:s % 2 + 1], psum_all[:, b0:b0 + w], AX, ALU.max))
                    if s >= 2:
                        ve.wait_ge(sm["p_exp"], s - 1)
                    V.tensor_scalar(nbias[:, s % 2:s % 2 + 1], nmax[:, s % 2:s % 2 + 1], -ATT_SCALE, None, ALU.mult).then_inc(sm["nb_ok"], 1)
                if h + 1 < MH and qb < FILLED:
                    pj_low(h + 1, qb)
                if 1 <= s <= STEPS:
                    p = s - 1
                    wp = (p % TT + 1) * P
                    ve.wait_ge(sm["p_exp"], p + 1)
                    op(V.reciprocal(prec[:, p % 2:p % 2 + 1], psums[:, p % 2:p % 2 + 1]))
                    V.tensor_scalar(p_sb[p % 3][:, 0:wp], p_sb[p % 3][:, 0:wp], prec[:, p % 2:p % 2 + 1], None, ALU.mult).then_inc(sm["p_norm"], 1)
                if s >= 2:
                    p = s - 2
                    pq = p % TT
                    for g in range(1 if pq < 4 else 2):
                        tg = tgroup(p, g)
                        n = min(pq + 1 - 4 * g, 4)
                        ve.wait_ge(sm["pt_hi"], tg + 1)
                        c = slice(pq % 4 * P, (pq % 4 + 1) * P)
                        split_lo(pT_lo[:, 4 * g:4 * g + n, c], psum[4 + tg % 2][:, 0:n * P].rearrange("p (a b) -> p a b", a=n),
                                 pT_hi[:, 4 * g:4 * g + n, c]).then_inc(sm["pt_lo"], 1)
                if s in EARLY:
                    k = EARLY[s]
                    m = early.index(k)
                    ve.wait_ge(sm["vd2"], m + 1)
                    split_lo(mT[k][1][:, :], ld2[m % 2][:, :], mT[k][0][:, :]).then_inc(sm["ad2"], 1)

            ve.wait_ge(sm["vd2"], KT)
            split_lo(mT[7][1][:, 0:HALF], om_st[0][:, :], mT[7][0][:, 0:HALF]).then_inc(sm["ad2"], 1)
            ve.wait_ge(sm["vd2"], KT + 1)
            split_lo(mT[7][1][:, HALF:S], psum[6], mT[7][0][:, HALF:S]).then_inc(sm["ad2"], 1)
            for g in range(17):
                if g < 16:
                    ve.wait_ge(sm["mo_mm"], g + 1)
                    ve.wait_ge(mx_in[g % 2], 32 * (g // 2 + 1))
                    if g >= 2:
                        ve.wait_ge(sm["mix_lo"], g - 1)
                    V.tensor_tensor(mx[g % 2][:, :], psum[g % 4], sgb_st[g % 2][:, :], ALU.mult).then_inc(sm["mo_ev"], 1)
                    ve.wait_ge(sm["mo_ev"], g + 1)
                    V.tensor_tensor(mx[g % 2][:, :], mx[g % 2][:, :], mm_st[g % 2][:, :], ALU.add).then_inc(sm["mix_ok"], 1)
                if g >= 1:
                    f, hs = (g - 1) // 2, slice((g - 1) % 2 * HALF, ((g - 1) % 2 + 1) * HALF)
                    ve.wait_ge(sm["mix_hi"], g)
                    split_lo(xm_lo[:, f, hs], mx[(g - 1) % 2][:, :], xm_hi[:, f, hs]).then_inc(sm["mix_lo"], 1)

            def row_stats(rows, stats, t, dh):
                vc.done(V.bn_stats(stats[:, t, 6 * dh:6 * dh + 6], rows[:, t, dh * HALF:(dh + 1) * HALF]))

            def row_var(stats, mvt, rst, t, sem_v):
                vc.wait()
                op(V.bn_aggr(mvt[:, t, :], stats[:, t, :]))
                V.tensor_scalar(rst[:, t, 0:1], mvt[:, t, 1:2], LN_EPS, None, ALU.add).then_inc(sem_v, 1)

            def row_scale(mvt, rst, t, sem_s, sem_r):
                ve.wait_ge(sem_s, t + 1)
                op(V.reciprocal(rst[:, t, 1:2], rst[:, t, 0:1]))
                V.scalar_tensor_tensor(rst[:, t, 2:3], mvt[:, t, 0:1], -1.0, rst[:, t, 1:2], ALU.mult, ALU.mult).then_inc(sem_r, 1)

            for dh in range(2):
                for t in range(TT):
                    c = slice(dh * HALF, (dh + 1) * HALF)
                    ve.wait_ge(row_in[t], 16)
                    ve.wait_ge(sm["wo_mm"], dh * TT + t + 1)
                    V.scalar_tensor_tensor(h_tok[:, t, c], h_tok[:, t, c], ALPHA, psum[t], ALU.mult, ALU.add).then_inc(sm["wo_ev"], 1)
                    ve.wait_ge(sm["wo_ev"], dh * TT + t + 1)
                    row_stats(h_tok, bst, t, dh)
                    if dh == 1:
                        row_var(bst, mv, lrs, t, sm["ln_v"])
                        if t >= 1:
                            row_scale(mv, lrs, t - 1, sm["ln_s"], sm["ln_r"])
            row_scale(mv, lrs, TT - 1, sm["ln_s"], sm["ln_r"])
            for i in range(2 * KT):
                half, k = divmod(i, KT)
                hs = slice(half * HALF, (half + 1) * HALF)
                ve.wait_ge(sm["hT_hi"], i + 1)
                op(V.tensor_scalar(y_st[i % 2][:, :], psum[4 + i % 4], ln_cols[:, 0, k:k + 1], ln_cols[:, 1, k:k + 1], ALU.mult, ALU.add))
                split_lo(hT_lo[:, k, hs], y_st[i % 2][:, :], hT_hi[:, k, hs]).then_inc(sm["hT_lo"], 1)
            ve.wait_ge(ln1_in, 32)
            ve.wait_ge(sm["hT_mm"], 2 * KT)

            def conv(dst, b0, half, fcol, done):
                c0 = half * HALF
                lo = 1 if half == 0 else 0
                op(V.scalar_tensor_tensor(dst[:, lo:HALF], psum_all[:, b0 + c0 + lo - 1:b0 + c0 + HALF - 1], cw[:, 1, fcol:fcol + 1],
                                          dst[:, lo:HALF], ALU.mult, ALU.add))
                lo = 2 if half == 0 else 0
                V.scalar_tensor_tensor(dst[:, lo:HALF], psum_all[:, b0 + c0 + lo - 2:b0 + c0 + HALF - 2], cw[:, 0, fcol:fcol + 1],
                                       dst[:, lo:HALF], ALU.mult, ALU.add).then_inc(sm["up_c"], 1)

            for i in range(FT):
                if i < TT:
                    op(V.tensor_tensor(h_tok[:, i, :], h_tok[:, i, :], ln_g[:, :], ALU.mult))
                    V.tensor_tensor(h_tok[:, i, :], h_tok[:, i, :], ln_b[:, :], ALU.add).then_inc(sm["ln_ok"], 1)
                b0 = 4 * (i % 2) * HALF
                for half in range(2):
                    n = 2 * i + half
                    ve.wait_ge(sm["up_a"], 2 * n + 1)
                    conv(up_g, b0, half, i, None)
                    ve.wait_ge(sm["up_a"], 2 * n + 2)
                    conv(up_v, b0 + 2 * HALF, half, FT + i, None)
                    ve.wait_ge(sm["up_c"], 2 * n + 2)
                    ve.wait_ge(sm["up_si"], n + 1)
                    V.tensor_tensor(f_all[:, FT - 1 - i, half * HALF:(half + 1) * HALF], up_g[:, :], up_v[:, :], ALU.mult).then_inc(sm["up_f"], 1)

            for i in range(FT):
                dh, kk = divmod(i, FT // 2)
                for k in range(2):
                    u = 2 * i + k
                    ve.wait_ge(sm["fs_hi"], u + 1)
                    split_lo(f_lo[u % 4][:, :], f_all[:, FT - 1 - (2 * kk + k), :], f_hi[u % 4][:, :]).then_inc(sm["fs_lo"], 1)
                if i == FT // 2:
                    for t in range(TT):
                        ve.wait_ge(row2_in[t], 16)
                        ve.wait_ge(sm["dn_mm"], t + 1)
                        V.scalar_tensor_tensor(z_tok[:, t, 0:HALF], z_tok[:, t, 0:HALF], ALPHA, psum[t], ALU.mult, ALU.add).then_inc(sm["dn_ev"], 1)
                    ve.wait_ge(sm["dn_ev"], TT)
                    for t in range(TT):
                        row_stats(z_tok, bst2, t, 0)
            ve.wait_ge(ln2_in, 32)
            for t in range(TT + 2):
                if t < TT:
                    ve.wait_ge(sm["dn_mm"], TT + t + 1)
                    V.scalar_tensor_tensor(z_tok[:, t, HALF:D], z_tok[:, t, HALF:D], ALPHA, psum[t], ALU.mult, ALU.add).then_inc(sm["dn_ev"], 1)
                    ve.wait_ge(sm["dn_ev"], TT + t + 1)
                    row_stats(z_tok, bst2, t, 1)
                    row_var(bst2, mv2, lrs2, t, sm["ln2_v"])
                if 1 <= t <= TT:
                    row_scale(mv2, lrs2, t - 1, sm["ln2_s"], sm["ln2_r"])
                if t >= 2:
                    ve.wait_ge(sm["ln2_n"], t - 1)
                    V.tensor_tensor(z_tok[:, t - 2, :], z_tok[:, t - 2, :], ln2_gt[:, :], ALU.mult).then_inc(sm["ln2_g"], 1)

        @block.scalar
        def _(ac):
            A = nc.scalar
            sc = Chain(ac, as_)

            def op(ins):
                sc.done(ins)
                sc.wait()

            for k in range(3):
                ac.dma_start(cw_rows[:, k, :], conv_w[0, k].rearrange("(j p) -> j p", p=P)).then_inc(par_landed, 16)
            ac.dma_start(cw_rows[:, 3, :], conv_b[0].rearrange("(j p) -> j p", p=P)).then_inc(par_landed, 16)
            ac.dma_start(w_gate[:, :], gla_w_gate_up[0]).then_inc(par_landed, 16)
            with nc.allow_non_contiguous_dma("a few hundred parameters, once"):
                ac.dma_start(b_gate[:, :], gla_b_gate[0].rearrange("(j p) -> p j", p=P)).then_inc(par_landed, 16)
                ac.dma_start(norm_g[:, :], gla_norm_g[0].rearrange("(j p) -> p j", p=P)).then_inc(par_landed, 16)
                ac.dma_start(lat_g[:, 0:QKT], mla_q_norm_g[0].rearrange("(j p) -> p j", p=P)).then_inc(par_landed, 16)
                ac.dma_start(ln_cols[:, 0, :], ln1_g[0].rearrange("(j p) -> p j", p=P)).then_inc(par_landed, 16)
                ac.dma_start(ln_cols[:, 1, :], ln1_b[0].rearrange("(j p) -> p j", p=P)).then_inc(par_landed, 16)
                ac.dma_start(lat_g[:, QKT:], mla_kv_norm_g[0].rearrange("(j p) -> p j", p=P)).then_inc(par_landed, 16)
            for i in range(2 * TT):
                t, g = divmod(i, 2)
                ac.wait_ge(xt_done, i + 1)
                A.copy(xT_hi[:, 4 * g:4 * g + 4, t * P:(t + 1) * P], psum[i % 4].rearrange("p (a b) -> p a b", a=4)).then_inc(xt_hi, 1)
            ac.wait_ge(par_landed, 16 * PARAMS)

            sig_users = []
            stored = [0, 0]

            def stage():
                u = len(sig_users)
                if u >= 2:
                    ac.wait_ge(*sig_users[u - 2])
                return u

            def got(kind):
                ac.wait_ge(mm, gid[kind] + 1)
                return bank(kind)

            def og_group(h, j):
                u = stage()
                b = got(("og", h, j))
                A.activation(sig[u % 2][:, :], b, ACT.Sigmoid).then_inc(sm["sig_ok"], 1)
                sig_users.append(ev_at[gid[("og", h, j)]])

            def gate_group(kind, dst):
                name, c, j = kind
                u = stage()
                b = got(kind)
                A.activation(sig[u % 2][:, :], b, ACT.Sigmoid).then_inc(ev_a, 1)
                ac.wait_ge(*ev_at[gid[kind]])
                f = 2 * c + j // 2
                stored[u % 2] += 16
                ac.dma_start(dst[f * P:(f + 1) * P, j % 2 * HALF:(j % 2 + 1) * HALF], sig[u % 2][:, :]).then_inc(sig_st[u % 2], 16)
                sig_users.append((sig_st[u % 2], stored[u % 2]))

            def v_group(h, j):
                A.copy(v_tok[h % 2][:, 2 * j:2 * j + 2, :], got(("v", h, j)).rearrange("p (a b) -> p a b", a=2)).then_inc(ev_a, 1)

            def gates(h):
                ac.wait_ge(sm["gate_mm"], h + 1)
                if h >= 1:
                    ac.wait_ge(sm["prep_done"], h)
                for half in range(2):
                    hs = slice(half * HALF, (half + 1) * HALF)
                    sc.done(A.activation(gb_b[:, hs], psum[4 + half], ACT.Identity, bias=b_gate[:, h:h + 1]))
                    sc.done(A.activation(gb_e[:, hs], psum[4 + half], ACT.Abs, bias=b_gate[:, h:h + 1]))
                sc.wait()
                op(A.activation(gb_e[:, :], gb_e[:, :], ACT.Exp, scale=-1.0))
                A.activation(gb_e[:, :], gb_e[:, :], ACT.Ln, bias=1.0).then_inc(sm["gate_l"], 1)
                ac.wait_ge(sm["gate_scan"], h + 1)
                sc.done(A.activation(gb_e[:, :], gb_b[:, :], ACT.Exp, scale=1.0 / TAU))
                sc.done(A.activation(gb_n[:, :], gb_n[:, :], ACT.Exp, scale=1.0 / TAU))
                sc.done(A.activation(dec[:, :], b_last[:, :], ACT.Exp, scale=1.0 / TAU))
                A.activation(gb_b[:, :], gb_b[:, :], ACT.Exp, scale=-1.0 / TAU).then_inc(sm["gate_exp"], 1)

            def qk_groups(h):
                for j in range(4):
                    dst, hs = (q_raw, k_raw)[j // 2], slice(j % 2 * HALF, (j % 2 + 1) * HALF)
                    A.copy(dst[:, hs], got(("qk", h, j))).then_inc(ev_a, 1)

            for half in range(2):
                A.copy(rT[:, half * HALF:(half + 1) * HALF], got(("r", half))[0:RANK, :]).then_inc(ev_a, 1)
            qk_groups(0)
            gates(0)
            for j in range(4):
                og_group(0, j)
            for j in range(4):
                v_group(0, j)
            for h in range(GH):
                last_head = h == GH - 1
                for t in range(TT):
                    i = h * TT + t
                    ac.wait_ge(sm["att_mm"], i + 1)
                    if i >= 2:
                        ac.wait_ge(sm["ou_mm"], i - 1)
                    A.copy(kst[i % 2][:, :], psum[7][:, 0:P]).then_inc(sm["kst_ok"], 1)
                    if last_head:
                        gate_group(("ga", t // 4, t % 4), d_sga)
                    elif t < 4:
                        og_group(h + 1, t)
                    else:
                        v_group(h + 1, t - 4)
                    ac.wait_ge(sm["ou_mm"], i + 1)
                    sc.done(A.copy(o_tok[:, t, :], psum[5][:, 0:DV]))
                    sc.wait()
                    A.activation(sq_junk[:, :], o_tok[:, t, :], ACT.Square, accum_out=small[:, t:t + 1]).then_inc(sm["o_ev"], 1)
                ac.wait_ge(sm["norm_v"], h + 1)
                A.activation(rs, rs, ACT.Sqrt).then_inc(sm["norm_s"], 1)
                if not last_head:
                    gates(h + 1)
                    qk_groups(h + 1)
                for j in range(4):
                    u = 4 * h + j
                    vt, half = divmod(j, 2)
                    ac.wait_ge(*ev_at[gid[("oT", h, j)]])
                    row = h * DV + vt * P
                    ac.dma_start(d_og[row:row + P, half * HALF:(half + 1) * HALF], oT_st[u % 2][:, :]).then_inc(oT_out[u % 2], 16)
                if not last_head:
                    for j in range(4):
                        gate_group(("gb", h, j), d_sgb)
            ac.wait_ge(oT_out[0], 16 * 8)
            ac.wait_ge(oT_out[1], 16 * 8)
            ac.wait_ge(sm["o_scaled"], GH)

            def op_load(k):
                ac.dma_start(ld_st[k % 2][:, :], d_og[k * P:(k + 1) * P, :]).then_inc(ld_in[k % 2], 16)

            op_load(0)
            op_load(1)
            after = {0: (0,), 1: (1, 2), 2: (3,), 3: (4, 5), 4: (6,), 5: (7,)}
            for j in range(8):
                gate_group(("ga", 2 + j // 4, j % 4), d_sga)
                for k in after.get(j, ()):
                    ac.wait_ge(ld_in[k % 2], 16 * (k // 2 + 1))
                    A.copy(oT_hi[:, k, :], ld_st[k % 2][:, :]).then_inc(sm["op_hi"], 1)
                    if k + 2 < KT:
                        ac.wait_ge(sm["op_lo"], k + 1)
                        op_load(k + 2)
            ac.wait_ge(sig_st[0], stored[0])
            ac.wait_ge(sig_st[1], stored[1])

            def ga_load(g):
                f, half = divmod(g, 2)
                ac.dma_start(ga_st[g % 2][:, :], d_sga[f * P:(f + 1) * P, half * HALF:(half + 1) * HALF]).then_inc(ga_in[g % 2], 16)

            ga_load(0)
            ga_load(1)
            for g in range(16):
                f, half = divmod(g, 2)
                kind = ("glao", g // 4, g % 4)
                ac.wait_ge(*ev_at[gid[kind]])
                ac.dma_start(d_m[f * P:(f + 1) * P, half * HALF:(half + 1) * HALF], m_st[g % 2][:, :]).then_inc(m_out[g % 2], 16)
                if g + 2 < 16:
                    ga_load(g + 2)
            ac.wait_ge(m_out[0], 16 * 8)
            ac.wait_ge(m_out[1], 16 * 8)
            with nc.allow_non_contiguous_dma("1024 positions, once"):
                ac.dma_start(pos_i[:, :], positions[0].rearrange("(t p) -> p t", p=P)).then_inc(sm["pos_ok"], 16)
            for j, (c0, c) in enumerate(LAT):
                for t in range(TT):
                    A.copy(c_tok[:, t, c0:c0 + c], got(("lat", j, t))[:, 0:c]).then_inc(ev_a, 1)
            ac.wait_ge(*ev_at[gid[("lat", 2, TT - 1)]])
            for t in range(TT):
                if t:
                    ac.wait_ge(sm["lat_sq"], 2 * t)
                A.activation(junk2[:, :], c_tok[:, t, 0:QR], ACT.Square, accum_out=small[:, 16 + t:17 + t]).then_inc(sm["lat_sq"], 1)
                ac.wait_ge(sm["lat_sq"], 2 * t + 1)
                A.activation(junk2[:, 0:KR], c_tok[:, t, QR:QR + KR], ACT.Square, accum_out=small[:, 24 + t:25 + t]).then_inc(sm["lat_sq"], 1)
            ac.wait_ge(sm["lat_v"], 1)
            A.activation(small[:, 16:32], small[:, 16:32], ACT.Sqrt).then_inc(sm["lat_s"], 1)
            ac.wait_ge(sm["angs"], 2)
            A.activation(sin[:, :, :], sin[:, :, :], ACT.Sin).then_inc(sm["sins"], 1)
            A.activation(cos[:, :, :], cos[:, :, :], ACT.Sin).then_inc(sm["sins"], 1)
            gs = [0, 0]
            for j in range(4):
                kind = ("gb", 3, j)
                b = got(kind)
                if j >= 2:
                    ac.wait_ge(sig_st[j % 2], stored[j % 2])
                A.activation(gsig2[j % 2][:, :], b, ACT.Sigmoid).then_inc(ev_a, 1)
                ac.wait_ge(*ev_at[gid[kind]])
                f = 6 + j // 2
                stored[j % 2] += 16
                ac.dma_start(d_sgb[f * P:(f + 1) * P, j % 2 * HALF:(j % 2 + 1) * HALF], gsig2[j % 2][:, :]).then_inc(sig_st[j % 2], 16)
            for c in range(QKT + KVT):
                for half in range(2):
                    A.activation(cT_hi[:, c, half * HALF:(half + 1) * HALF], got(("cT", c, half)), ACT.Copy, scale=lat_g[:, c:c + 1]).then_inc(sm["hi_ok"], 1)
            for m in range(2):
                for half in range(2):
                    A.copy((kA, kB)[m][:, half * HALF:(half + 1) * HALF], got(("kT", m, half))).then_inc(ev_a, 1)
            def pj_high(h, j):
                ac.wait_ge(sm["pj_mm"], 6 * h + j + 1)
                kind, half = divmod(j, 2)
                dst = (qT, kT, vv)[kind][h % 2]
                if kind < 2:
                    A.copy(dst[0][:, half * HALF:(half + 1) * HALF], psum[7]).then_inc(sm["pj_hi"], 1)
                else:
                    A.copy(dst[0][:, 4 * half:4 * half + 4, :], psum[7].rearrange("p (a b) -> p a b", a=4)).then_inc(sm["pj_hi"], 1)

            pj_high(0, 0)
            for t in range(TT):
                if t < 5:
                    pj_high(0, t + 1)
                for g in range(2):
                    b = got(("qrT", t, g))
                    if g == 0 and t >= 2:
                        ac.wait_ge(qs_out[t % 2], 16 * (t // 2))
                    A.copy(qr_st[t % 2][:, 4 * g:4 * g + 4, :], b.rearrange("p (a b) -> p a b", a=4)).then_inc(ev_a, 1)
                ac.wait_ge(*ev_at[gid[("qrT", t, 1)]])
                ac.dma_start(d_qr.rearrange("h p s -> p h s")[:, :, t * P:(t + 1) * P], qr_st[t % 2][:, :, :]).then_inc(qs_out[t % 2], 16)

            ac.wait_ge(qs_out[0], 16 * 4)
            ac.wait_ge(qs_out[1], 16 * 4)
            ac.wait_ge(sig_st[0], stored[0])
            ac.wait_ge(sig_st[1], stored[1])

            def qr_load(h):
                ac.dma_start(qrA[h % 2][:, :].bitcast(F32), d_qr[h]).then_inc(qrA_in[h % 2], 16)

            qr_load(0)

            def om_load(m):
                k = early[m]
                ac.wait_ge(om_out[0], 16 * (k + 1))
                ac.wait_ge(om_out[1], 16 * (k + 1))
                ac.dma_start(ld2[m % 2][:, :], d_om[k * P:(k + 1) * P, :]).then_inc(ld_in[m % 2], 16)

            def mix_load(g):
                f, hs = g // 2, slice(g % 2 * HALF, (g % 2 + 1) * HALF)
                ac.dma_start(sgb_st[g % 2][:, :], d_sgb[f * P:(f + 1) * P, hs]).then_inc(mx_in[g % 2], 16)
                ac.dma_start(mm_st[g % 2][:, :], d_m[f * P:(f + 1) * P, hs]).then_inc(mx_in[g % 2], 16)

            def probs_out(s):
                if 2 <= s < STEPS + 2:
                    p = s - 2
                    pq = p % TT
                    for g in range(1 if pq < 4 else 2):
                        tg = tgroup(p, g)
                        n = min(pq + 1 - 4 * g, 4)
                        ac.wait_ge(sm["t_mm"], tg + 1)
                        A.copy(pT_hi[:, 4 * g:4 * g + n, pq % 4 * P:(pq % 4 + 1) * P], psum[4 + tg % 2][:, 0:n * P].rearrange("p (a b) -> p a b", a=n)).then_inc(sm["pt_hi"], 1)

            def block_out(s):
                if s >= 3 and (s - 3) % 4 == 3:
                    n = (s - 3) // 4
                    ac.wait_ge(sm["pv_mm"], n + 1)
                    if n >= 2:
                        ac.wait_ge(om_out[n % 2], 16 * (n // 2))
                    if n == 2 * MH - 1:
                        return
                    A.copy(om_st[n % 2][:, :], psum[6]).then_inc(sm["om_ev"], 1)
                    ac.wait_ge(sm["om_ev"], n + 1)
                    if n < 2 * MH - 2:
                        ac.dma_start(d_om[n // 2 * MV:(n // 2 + 1) * MV, n % 2 * HALF:(n % 2 + 1) * HALF], om_st[n % 2][:, :]).then_inc(om_out[n % 2], 16)

            for s in range(STEPS + 3):
                h, qb = divmod(s, TT)
                if qb == 0 and h + 1 < MH:
                    if h >= 1:
                        ac.wait_ge(sm["s_mm"], TT * h)
                    qr_load(h + 1)
                if qb >= FILLED or h >= MH - 1:
                    block_out(s)
                    probs_out(s)
                if s < STEPS:
                    w = (qb + 1) * P
                    ac.wait_ge(sm["nb_ok"], s + 1)
                    if s >= 3:
                        ac.wait_ge(sm["t_mm"], tgroup(s - 3, 0 if (s - 3) % TT < 4 else 1) + 1)
                    if s >= 2:
                        ac.wait_ge(sm["p_norm"], s - 1)
                    A.activation(p_sb[s % 3][:, 0:w], psum_all[:, (s % 2) * S:(s % 2) * S + w], ACT.Exp, bias=nbias[:, s % 2:s % 2 + 1],
                                 scale=ATT_SCALE, accum_out=psums[:, s % 2:s % 2 + 1]).then_inc(sm["p_exp"], 1)
                if h + 1 < MH and qb < FILLED:
                    pj_high(h + 1, qb)
                if qb < FILLED and h < MH - 1:
                    block_out(s)
                    probs_out(s)
                if s == STEPS - TT:
                    ac.wait_ge(sm["s_mm"], STEPS - TT)
                    om_load(0)
                if s in EARLY:
                    k = EARLY[s]
                    m = early.index(k)
                    if m + 1 < len(early):
                        if m >= 1:
                            ac.wait_ge(sm["ad2"], m)
                        om_load(m + 1)
                    if k == 5:
                        ac.wait_ge(sm["s_mm"], STEPS)
                    ac.wait_ge(ld_in[m % 2], 16 * (4 + m // 2 + 1))
                    A.copy(mT[k][0][:, :], ld2[m % 2][:, :]).then_inc(sm["vd2"], 1)

            A.copy(mT[7][0][:, 0:HALF], om_st[0][:, :]).then_inc(sm["vd2"], 1)
            A.copy(mT[7][0][:, HALF:S], psum[6]).then_inc(sm["vd2"], 1)
            mix_load(0)
            mix_load(1)
            for g in range(16):
                ac.wait_ge(sm["mix_ok"], g + 1)
                A.copy(xm_hi[:, g // 2, g % 2 * HALF:(g % 2 + 1) * HALF], mx[g % 2][:, :]).then_inc(sm["mix_hi"], 1)
                if g + 2 < 16:
                    mix_load(g + 2)
            ac.wait_ge(sm["mo_mm"], 16)
            for t in range(TT):
                ac.dma_start(h_tok[:, t, :], x[0, t * P:(t + 1) * P, :]).then_inc(row_in[t], 16)
            ac.dma_start(ln_g[:, :], ln1_g[0].partition_broadcast(P)).then_inc(ln1_in, 16)
            ac.dma_start(ln_b[:, :], ln1_b[0].partition_broadcast(P)).then_inc(ln1_in, 16)
            def row_norms(rows, rst, t, names):
                v, s_, r_, n_ = (sm[x] for x in names)
                if t < TT:
                    ac.wait_ge(v, t + 1)
                    A.activation(rst[:, t, 0:1], rst[:, t, 0:1], ACT.Sqrt).then_inc(s_, 1)
                if t >= 1:
                    ac.wait_ge(r_, t)
                    A.activation(rows[:, t - 1, :], rows[:, t - 1, :], ACT.Identity, bias=rst[:, t - 1, 2:3], scale=rst[:, t - 1, 1:2]).then_inc(n_, 1)

            for t in range(TT + 1):
                row_norms(h_tok, lrs, t, ("ln_v", "ln_s", "ln_r", "ln_n"))
            for i in range(2 * KT):
                half, k = divmod(i, KT)
                ac.wait_ge(sm["hT_mm"], i + 1)
                A.activation(hT_hi[:, k, half * HALF:(half + 1) * HALF], psum[4 + i % 4], ACT.Identity,
                             bias=ln_cols[:, 1, k:k + 1], scale=ln_cols[:, 0, k:k + 1]).then_inc(sm["hT_hi"], 1)
            for i in range(FT):
                if i < TT:
                    ac.wait_ge(sm["ln_ok"], i + 1)
                    ac.dma_start(d_h[i * P:(i + 1) * P, :], h_tok[:, i, :]).then_inc(sm["h_stored"], 16)
                if i == TT:
                    ac.wait_ge(sm["h_stored"], 16 * TT)
                for half in range(2):
                    n = 2 * i + half
                    for part, dst in ((0, up_g), (1, up_v)):
                        b = 4 * (i % 2) + 2 * part + half
                        ac.wait_ge(sm["up_mm"], 4 * i + 2 * half + part + 1)
                        if n >= 1:
                            ac.wait_ge(sm["up_f"], n)
                        fc = part * FT + i
                        A.activation(dst[:, :], psum[b], ACT.Identity, bias=cw[:, 3, fc:fc + 1], scale=cw[:, 2, fc:fc + 1]).then_inc(sm["up_a"], 1)
                    ac.wait_ge(sm["up_c"], 2 * n + 1)
                    A.activation(up_g[:, :], up_g[:, :], ACT.Silu).then_inc(sm["up_si"], 1)
            ac.wait_ge(sm["up_mm"], 4 * FT)
            for i in range(FT):
                kk = i % (FT // 2)
                if i >= 2:
                    ac.wait_ge(*used_at(slot_no[("down", i - 2)]))
                    ac.wait_ge(sm["fs_lo"], 2 * i - 2)
                for k in range(2):
                    u = 2 * i + k
                    A.copy(f_hi[u % 4][:, :], f_all[:, FT - 1 - (2 * kk + k), :]).then_inc(sm["fs_hi"], 1)
                if i == 0:
                    for t in range(TT):
                        ac.dma_start(z_tok[:, t, :], d_h[t * P:(t + 1) * P, :]).then_inc(row2_in[t], 16)
                if i == FT // 2 + 1:
                    ac.wait_ge(sm["fs_lo"], FT + 2)
                    ac.wait_ge(sm["fs_hi"], FT + 2)
                    ac.dma_start(ln2_gt[:, :], ln2_g[0].partition_broadcast(P)).then_inc(ln2_in, 16)
                    ac.dma_start(ln2_bt[:, :], ln2_b[0].partition_broadcast(P)).then_inc(ln2_in, 16)
            for t in range(TT + 1):
                row_norms(z_tok, lrs2, t, ("ln2_v", "ln2_s", "ln2_r", "ln2_n"))
                if t >= 4:
                    ac.wait_ge(sm["ln2_ok"], t - 3)
                    ac.dma_start(out[0, (t - 4) * P:(t - 3) * P, :], z_tok[:, t - 4, :]).then_inc(sm["out_stored"], 16)
            for t in range(TT - 3, TT):
                ac.wait_ge(sm["ln2_ok"], t + 1)
                ac.dma_start(out[0, t * P:(t + 1) * P, :], z_tok[:, t, :]).then_inc(sm["out_stored"], 16)
            ac.wait_ge(sm["out_stored"], 16 * TT)


_INS = ["x", "positions", "w_in", "gla_w_gate_up", "gla_b_gate", "gla_norm_g", "w_gla_o", "mla_q_norm_g", "mla_w_uq",
        "mla_kv_norm_g", "mla_w_ukv", "w_mla_o", "w_out", "ln1_g", "ln1_b", "w_up", "conv_w", "conv_b", "w_down",
        "ln2_g", "ln2_b"]


def kernel(**inputs):
    import numpy as _np
    import concourse.bacc as _bacc
    from concourse import mybir as _mybir
    from concourse.bass_utils import run_bass_kernel_spmd as _run

    nc = _bacc.Bacc("TRN2", target_bir_lowering=False, num_devices=1)
    arrays, args = {}, []
    for name in _INS:
        a = _np.ascontiguousarray(inputs[name])
        arrays[f"in_{name}_dram"] = a
        args.append(nc.dram_tensor(f"in_{name}_dram", a.shape, _mybir.dt.from_np(a.dtype), kind="ExternalInput").ap())
    out = nc.dram_tensor("out_0_dram", (1, S, D), F32, kind="ExternalOutput").ap()
    block_kernel(nc, *args, out)
    r = _run(nc, [arrays], core_ids=[0])
    return r.results[0]["out_0_dram"]
```
